# Optimizing a Trainium2 kernel written in Bass

```python
import numpy as np
import jax, jax.numpy as jnp
from jax import lax

D_MODEL = 1024
BATCH = 1
SEQ = 512
DEPTH = 2

D_FF = 2816
RMS_EPS = 1e-6
ROPE_THETA = 10000.0
CHUNK = 64

GLA_H = 4
GLA_DK = 64
GLA_DV = 128
GLA_RANK = 16
GLA_GATE_NORM = 16.0

NSA_H = 8
NSA_G = 2
NSA_D = 64
CMP_LEN = 32
CMP_STRIDE = 16
CMP_HIDDEN = 256
SLC_LEN = 64
SLC_TOPK = 16
WIN = 512
Q_BLOCK = 128
FORCED_SCORE = 1e4

MLSTM_H = 4
MLSTM_DK = 64
MLSTM_DV = 128
CONV_W = 4

MIX_W = 512
N_BRANCH = 3

IN_SIZES = (
    GLA_H * GLA_DK, GLA_H * GLA_DK, GLA_H * GLA_DV, GLA_H * GLA_DV, GLA_RANK,
    NSA_H * NSA_D,
    NSA_G * NSA_D, NSA_G * NSA_D,
    NSA_G * NSA_D, NSA_G * NSA_D,
    NSA_G * NSA_D, NSA_G * NSA_D,
    NSA_H * 3,
    2 * MLSTM_H * MLSTM_DK, MLSTM_H * MLSTM_DV, MLSTM_H * MLSTM_DV, MLSTM_H, MLSTM_H,
    D_MODEL, D_MODEL, D_MODEL,
)
N_IN = sum(IN_SIZES)

kernel_name = "hybrid_gla_nsa_mlstm_macaron"

def rms_norm(x, g):
    xf = x.astype(jnp.float32)
    y = xf * lax.rsqrt(jnp.mean(xf * xf, axis=-1, keepdims=True) + RMS_EPS)
    return (y * g.astype(jnp.float32)).astype(x.dtype)

def rope(x, pos):
    half = x.shape[-1] // 2
    freqs = ROPE_THETA ** (-jnp.arange(half, dtype=jnp.float32) / half)
    ang = pos.astype(jnp.float32)[:, None] * freqs[None, :]
    cos = jnp.cos(ang)[:, None, :]
    sin = jnp.sin(ang)[:, None, :]
    xf = x.astype(jnp.float32)
    x1, x2 = xf[..., :half], xf[..., half:]
    return jnp.concatenate([x1 * cos - x2 * sin, x1 * sin + x2 * cos], axis=-1).astype(x.dtype)

def swiglu(x, w_gate, w_up, w_down):
    return (jax.nn.silu(x @ w_gate) * (x @ w_up)) @ w_down

def masked_softmax(s, mask):
    s = jnp.where(mask, s.astype(jnp.float32), -jnp.inf)
    m = jnp.max(s, axis=-1, keepdims=True)
    m = jnp.where(jnp.isfinite(m), m, 0.0)
    p = jnp.exp(s - m)
    return p / jnp.maximum(jnp.sum(p, axis=-1, keepdims=True), 1e-30)

def split_columns(z):
    parts, off = [], 0
    for w in IN_SIZES:
        parts.append(z[..., off:off + w])
        off += w
    return parts

def to_chunks(t):
    B, S, H, d = t.shape
    return t.reshape(B, S // CHUNK, CHUNK, H, d).transpose(1, 0, 3, 2, 4)

def from_chunks(t):
    C, B, H, L, d = t.shape
    return t.transpose(1, 0, 3, 2, 4).reshape(B, C * L, H, d)

def causal_conv(x, w, b):
    K, C = w.shape
    y = lax.conv_general_dilated(x, w[:, None, :].astype(x.dtype), window_strides=(1,),
                                 padding=[(K - 1, 0)], dimension_numbers=('NWC', 'WIO', 'NWC'),
                                 feature_group_count=C)
    return y + b

def gla_chunked(q, k, v, log_alpha):
    B, S, H, DK = q.shape
    DV = v.shape[-1]
    f32 = jnp.float32
    qc = to_chunks(q.astype(f32) * DK ** -0.5)
    kc = to_chunks(k.astype(f32))
    vc = to_chunks(v.astype(f32))
    gc = to_chunks(log_alpha.astype(f32))
    causal = jnp.tril(jnp.ones((CHUNK, CHUNK), dtype=bool))

    def step(state, xs):
        q_i, k_i, v_i, g_i = xs
        b = jnp.cumsum(g_i, axis=2)
        o_inter = jnp.einsum('bhld,bhde->bhle', q_i * jnp.exp(b), state)
        diff = jnp.where(causal[:, :, None], b[:, :, :, None, :] - b[:, :, None, :, :], -jnp.inf)
        attn = jnp.einsum('bhid,bhjd,bhijd->bhij', q_i, k_i, jnp.exp(diff))
        b_last = b[:, :, -1:, :]
        k_dec = k_i * jnp.exp(b_last - b)
        state = jnp.exp(b_last[:, :, 0, :, None]) * state + jnp.einsum('bhld,bhle->bhde', k_dec, v_i)
        return state, o_inter + jnp.einsum('bhij,bhje->bhie', attn, v_i)

    state0 = jnp.zeros((B, H, DK, DV), f32)
    _, o = lax.scan(step, state0, (qc, kc, vc, gc))
    return from_chunks(o)

def mlstm_chunked(q, k, v, i_pre, log_f):
    B, S, H, DK = q.shape
    DV = v.shape[-1]
    f32 = jnp.float32
    qc = to_chunks(q.astype(f32))
    kc = to_chunks(k.astype(f32) * DK ** -0.5)
    vc = to_chunks(v.astype(f32))
    ic = to_chunks(i_pre.astype(f32)[..., None])[..., 0]
    fc = to_chunks(log_f.astype(f32)[..., None])[..., 0]
    causal = jnp.tril(jnp.ones((CHUNK, CHUNK), dtype=bool))

    def step(carry, xs):
        c_st, n_st, m_st = carry
        q_i, k_i, v_i, ii, fi = xs
        b = jnp.cumsum(fi, axis=-1)
        dmat = jnp.where(causal, b[..., :, None] - b[..., None, :] + ii[..., None, :], -jnp.inf)
        inter_log = b + m_st[..., None]
        m_row = jnp.maximum(inter_log, jnp.max(dmat, axis=-1))
        w_inter = jnp.exp(inter_log - m_row)
        s_qk = jnp.einsum('bhid,bhjd->bhij', q_i, k_i) * jnp.exp(dmat - m_row[..., None])
        num = w_inter[..., None] * jnp.einsum('bhld,bhde->bhle', q_i, c_st) + jnp.einsum('bhij,bhje->bhie', s_qk, v_i)
        den = w_inter * jnp.einsum('bhld,bhd->bhl', q_i, n_st) + jnp.sum(s_qk, axis=-1)
        h = num / jnp.maximum(jnp.abs(den), jnp.exp(-m_row))[..., None]
        m_new = m_row[..., -1]
        w_k = jnp.exp(dmat[..., -1, :] - m_new[..., None])
        decay = jnp.exp(b[..., -1] + m_st - m_new)
        c_new = decay[..., None, None] * c_st + jnp.einsum('bhld,bhle->bhde', k_i * w_k[..., None], v_i)
        n_new = decay[..., None] * n_st + jnp.einsum('bhl,bhld->bhd', w_k, k_i)
        return (c_new, n_new, m_new), h

    carry0 = (jnp.zeros((B, H, DK, DV), f32), jnp.zeros((B, H, DK), f32), jnp.zeros((B, H), f32))
    _, h = lax.scan(step, carry0, (qc, kc, vc, ic, fc))
    return from_chunks(h)

def nsa_attention(q, k_cmp, v_cmp, k_slc, v_slc, k_win, v_win, gates, qk_norm, cmp_pos, cmp_w1, cmp_w2):
    B, S, H, D = q.shape
    G = NSA_G
    HPG = H // G
    pos = jnp.arange(S)
    scale = D ** -0.5
    q = rope(rms_norm(q, qk_norm[0]), pos)
    k_slc = rope(rms_norm(k_slc, qk_norm[2]), pos)
    k_win = rope(rms_norm(k_win, qk_norm[3]), pos)

    n_cmp = S // CMP_STRIDE - 1

    def compress(t, pe, w1, w2):
        tb = t.reshape(B, S // CMP_STRIDE, CMP_STRIDE, G, D)
        blocks = jnp.concatenate([tb[:, :-1], tb[:, 1:]], axis=2) + pe[None, None, :, None, :]
        flat = blocks.transpose(0, 1, 3, 2, 4).reshape(B, n_cmp, G, CMP_LEN * D)
        return jax.nn.gelu(flat @ w1) @ w2

    cmp_end = jnp.arange(n_cmp) * CMP_STRIDE + CMP_LEN - 1
    kc = rope(rms_norm(compress(k_cmp, cmp_pos[0], cmp_w1[0], cmp_w2[0]), qk_norm[1]), cmp_end)
    vc = compress(v_cmp, cmp_pos[1], cmp_w1[1], cmp_w2[1])

    n_sel = S // SLC_LEN
    topk = min(SLC_TOPK, n_sel)
    ks_blk = k_slc.reshape(B, n_sel, SLC_LEN, G, D).transpose(0, 3, 1, 2, 4)
    vs_blk = v_slc.reshape(B, n_sel, SLC_LEN, G, D).transpose(0, 3, 1, 2, 4)
    ci = np.arange(n_cmp)[:, None] * CMP_STRIDE
    sj = np.arange(n_sel)[None, :] * SLC_LEN
    overlap = jnp.asarray(((ci < sj + SLC_LEN) & (ci + CMP_LEN > sj)).astype(np.float32))
    take = jax.vmap(jax.vmap(lambda kb, ix: kb[ix]))

    kw_pad = jnp.pad(k_win, ((0, 0), (WIN, 0), (0, 0), (0, 0)))
    vw_pad = jnp.pad(v_win, ((0, 0), (WIN, 0), (0, 0), (0, 0)))

    def block(qb):
        s0 = qb * Q_BLOCK
        t = s0 + jnp.arange(Q_BLOCK)
        qq = lax.dynamic_slice_in_dim(q, s0, Q_BLOCK, axis=1).reshape(B, Q_BLOCK, G, HPG, D)
        gg = lax.dynamic_slice_in_dim(gates, s0, Q_BLOCK, axis=1).reshape(B, Q_BLOCK, G, HPG, 3)
        sc = jnp.einsum('bqghd,bcgd->bghqc', qq, kc) * scale
        p_c = masked_softmax(sc, cmp_end[None, :] <= t[:, None])
        o_c = jnp.einsum('bghqc,bcgd->bqghd', p_c, vc)
        imp = jnp.einsum('bghqc,cn->bgqn', p_c, overlap)
        blk = jnp.arange(n_sel)[None, :]
        valid = blk * SLC_LEN <= t[:, None]
        cur = (t // SLC_LEN)[:, None]
        forced = (blk == 0) | (blk == cur) | (blk == cur - 1)
        score = jnp.where(valid, jnp.where(forced, FORCED_SCORE, imp), -jnp.inf)
        top_val, top_idx = lax.top_k(score, topk)
        k_sel = take(ks_blk, top_idx).reshape(B, G, Q_BLOCK, topk * SLC_LEN, D)
        v_sel = take(vs_blk, top_idx).reshape(B, G, Q_BLOCK, topk * SLC_LEN, D)
        tok = (top_idx[..., None] * SLC_LEN + jnp.arange(SLC_LEN)).reshape(B, G, Q_BLOCK, topk * SLC_LEN)
        m_s = jnp.repeat(jnp.isfinite(top_val), SLC_LEN, axis=-1) & (tok <= t[:, None])
        ss = jnp.einsum('bqghd,bgqnd->bghqn', qq, k_sel) * scale
        p_s = masked_softmax(ss, m_s[:, :, None])
        o_s = jnp.einsum('bghqn,bgqnd->bqghd', p_s, v_sel)
        kw = lax.dynamic_slice_in_dim(kw_pad, s0, WIN + Q_BLOCK, axis=1)
        vw = lax.dynamic_slice_in_dim(vw_pad, s0, WIN + Q_BLOCK, axis=1)
        kpos = s0 - WIN + jnp.arange(WIN + Q_BLOCK)
        m_w = (kpos[None, :] <= t[:, None]) & (kpos[None, :] > t[:, None] - WIN) & (kpos[None, :] >= 0)
        sw = jnp.einsum('bqghd,bkgd->bghqk', qq, kw) * scale
        p_w = masked_softmax(sw, m_w)
        o_w = jnp.einsum('bghqk,bkgd->bqghd', p_w, vw)
        o = gg[..., 0:1] * o_c + gg[..., 1:2] * o_s + gg[..., 2:3] * o_w
        return o.reshape(B, Q_BLOCK, H * D)

    out = lax.map(block, jnp.arange(S // Q_BLOCK))
    return out.transpose(1, 0, 2, 3).reshape(B, S, H * D)

def hybrid_mixer(h, w_in, b_in, gla_w_alpha, gla_b_alpha, gla_out_norm, nsa_qk_norm, nsa_cmp_pos,
                 nsa_cmp_w1, nsa_cmp_w2, mlstm_conv_w, mlstm_conv_b, w_branch, w_out):
    B, S, _ = h.shape
    f32 = jnp.float32
    z = h @ w_in + b_in
    (a_q, a_k, a_v, a_r, a_lr, b_q, b_kc, b_vc, b_ks, b_vs, b_kw, b_vw, b_g,
     c_qk, c_v, c_o, c_i, c_f, gate_a, gate_b, gate_c) = split_columns(z)

    def heads(t, n):
        return t.reshape(B, S, n, -1)

    log_alpha = jax.nn.log_sigmoid((a_lr @ gla_w_alpha + gla_b_alpha).astype(f32)) / GLA_GATE_NORM
    o_a = gla_chunked(heads(a_q, GLA_H), heads(a_k, GLA_H), heads(a_v, GLA_H), heads(log_alpha, GLA_H))
    o_a = rms_norm(o_a, gla_out_norm) * jax.nn.silu(heads(a_r, GLA_H).astype(f32))
    o_a = o_a.reshape(B, S, MIX_W).astype(h.dtype)

    o_b = nsa_attention(heads(b_q, NSA_H), heads(b_kc, NSA_G), heads(b_vc, NSA_G), heads(b_ks, NSA_G),
                        heads(b_vs, NSA_G), heads(b_kw, NSA_G), heads(b_vw, NSA_G),
                        heads(jax.nn.sigmoid(b_g), NSA_H), nsa_qk_norm, nsa_cmp_pos, nsa_cmp_w1, nsa_cmp_w2)
    o_b = o_b.astype(h.dtype)

    qk = jax.nn.silu(causal_conv(c_qk, mlstm_conv_w, mlstm_conv_b))
    c_q, c_k = qk[..., :MLSTM_H * MLSTM_DK], qk[..., MLSTM_H * MLSTM_DK:]
    h_c = mlstm_chunked(heads(c_q, MLSTM_H), heads(c_k, MLSTM_H), heads(c_v, MLSTM_H),
                        c_i, jax.nn.log_sigmoid(c_f.astype(f32)))
    o_c = (h_c.reshape(B, S, MIX_W) * jax.nn.sigmoid(c_o.astype(f32))).astype(h.dtype)

    y = (jax.nn.sigmoid(gate_a) * (o_a @ w_branch[0])
         + jax.nn.sigmoid(gate_b) * (o_b @ w_branch[1])
         + jax.nn.sigmoid(gate_c) * (o_c @ w_branch[2]))
    return y @ w_out

def setup_inputs(seed: int = 0) -> dict:
    key = jax.random.key(seed)
    ks = jax.random.split(key, 23)
    L, D, F = DEPTH, D_MODEL, D_FF
    f32 = jnp.float32

    def nrm(k, shape, scale):
        return jax.random.normal(k, shape, f32) * scale

    def gain(k, shape):
        return 1.0 + 0.02 * jax.random.normal(k, shape, f32)

    f_start = N_IN - 3 * D_MODEL - MLSTM_H
    b_in = nrm(ks[7], (L, N_IN), 0.02)
    b_in = b_in.at[:, f_start:f_start + MLSTM_H].add(jnp.linspace(3.0, 6.0, MLSTM_H, dtype=f32))
    return {
        'x': jax.random.normal(ks[0], (BATCH, SEQ, D), f32),
        'ffn1_norm': gain(ks[1], (L, D)),
        'ffn1_w_gate': nrm(ks[2], (L, D, F), D ** -0.5),
        'ffn1_w_up': nrm(ks[3], (L, D, F), D ** -0.5),
        'ffn1_w_down': nrm(ks[4], (L, F, D), F ** -0.5),
        'mix_norm': gain(ks[5], (L, D)),
        'w_in': nrm(ks[6], (L, D, N_IN), D ** -0.5),
        'b_in': b_in,
        'gla_w_alpha': nrm(ks[8], (L, GLA_RANK, GLA_H * GLA_DK), GLA_RANK ** -0.5),
        'gla_b_alpha': nrm(ks[9], (L, GLA_H * GLA_DK), 0.1),
        'gla_out_norm': gain(ks[10], (L, GLA_DV)),
        'nsa_qk_norm': gain(ks[11], (L, 4, NSA_D)),
        'nsa_cmp_pos': nrm(ks[12], (L, 2, CMP_LEN, NSA_D), 0.1),
        'nsa_cmp_w1': nrm(ks[13], (L, 2, CMP_LEN * NSA_D, CMP_HIDDEN), (CMP_LEN * NSA_D) ** -0.5),
        'nsa_cmp_w2': nrm(ks[14], (L, 2, CMP_HIDDEN, NSA_D), CMP_HIDDEN ** -0.5),
        'mlstm_conv_w': nrm(ks[15], (L, CONV_W, 2 * MLSTM_H * MLSTM_DK), CONV_W ** -0.5),
        'mlstm_conv_b': nrm(ks[16], (L, 2 * MLSTM_H * MLSTM_DK), 0.02),
        'w_branch': nrm(ks[17], (L, N_BRANCH, MIX_W, D), MIX_W ** -0.5),
        'w_out': nrm(ks[18], (L, D, D), D ** -0.5),
        'ffn2_norm': gain(ks[19], (L, D)),
        'ffn2_w_gate': nrm(ks[20], (L, D, F), D ** -0.5),
        'ffn2_w_up': nrm(ks[21], (L, D, F), D ** -0.5),
        'ffn2_w_down': nrm(ks[22], (L, F, D), F ** -0.5),
    }

def reference(x, ffn1_norm, ffn1_w_gate, ffn1_w_up, ffn1_w_down, mix_norm, w_in, b_in, gla_w_alpha,
              gla_b_alpha, gla_out_norm, nsa_qk_norm, nsa_cmp_pos, nsa_cmp_w1, nsa_cmp_w2, mlstm_conv_w,
              mlstm_conv_b, w_branch, w_out, ffn2_norm, ffn2_w_gate, ffn2_w_up, ffn2_w_down):
    for l in range(DEPTH):
        x = x + 0.5 * swiglu(rms_norm(x, ffn1_norm[l]), ffn1_w_gate[l], ffn1_w_up[l], ffn1_w_down[l])
        x = x + hybrid_mixer(rms_norm(x, mix_norm[l]), w_in[l], b_in[l], gla_w_alpha[l], gla_b_alpha[l],
                             gla_out_norm[l], nsa_qk_norm[l], nsa_cmp_pos[l], nsa_cmp_w1[l], nsa_cmp_w2[l],
                             mlstm_conv_w[l], mlstm_conv_b[l], w_branch[l], w_out[l])
        x = x + 0.5 * swiglu(rms_norm(x, ffn2_norm[l]), ffn2_w_gate[l], ffn2_w_up[l], ffn2_w_down[l])
    return x


_drawn_inputs = setup_inputs


def setup_inputs(seed=0):
    import zlib

    import numpy as np

    out = dict(_drawn_inputs(seed))
    spreads = {}
    factors = {'ffn1_norm': 3.661,
     'gla_b_alpha': 2.811,
     'gla_out_norm': 21.751,
     'nsa_qk_norm': 24.298,
     'ffn2_norm': 4.168,
     'nsa_cmp_pos': 2.695,
     'mlstm_conv_b': 38.517}
    for name, (base, spread) in spreads.items():
        noise = np.random.default_rng([zlib.crc32(name.encode()), seed]).standard_normal(out[name].shape)
        drawn = base * np.exp(spread * noise) if base else spread * noise
        out[name] = __import__('jax').numpy.asarray(drawn.astype(out[name].dtype))
    for name, factor in factors.items():
        out[name] = (out[name] * factor).astype(out[name].dtype)
    return out
```

```python
import concourse.bass as bass
from concourse import mybir
from contextlib import ExitStack

P = 128
L, S, DM, FF = 2, 512, 1024, 2816
KD, KF, NB = DM // P, FF // P, S // P
HD = 64
NCMP, CS = S // 16 - 1, 16
NH, NPAIR = 4, 4
GT_TILES = 12
W_SLOT = KF * P
EPS = 1e-6
DVE_STEPS = 183
LEVELS = [256, 128, 64, 32, 16, 8, 4, 2, 1]
SM, KC, VC, Q, KS, KW, VS, VW = 0, 1, 2, 3, 7, 8, 9, 10
R_F, R_I, R_LR, R_G = 0, 32, 64, 96
SECTIONS = [("gu0", KF), ("dn0", KD), ("pA", 6), ("cmp", 4), ("pB", 6), ("cb0", KD), ("pC", 6),
            ("cb1", KD), ("cb2", KD), ("wo", KD // 2), ("gu1", KF), ("dn1", KD)]
FIRST = {}
UNITS = 0
for _name, _n in SECTIONS:
    FIRST[_name] = UNITS
    UNITS += _n
WIDTHS = {"gu": (KD * P, KD * P), "dn": (KF // 2 * P, KF // 2 * P), "cb": (KD * P, 4 * P)}
COLS = {}
NPAR = 0
for _name, _n in [("norm", 3 * KD), ("bias", 3 * GT_TILES), ("gbias", 3 * KD), ("convw", 16), ("convb", 4),
                  ("qkn", 4), ("gn", 1), ("balpha", 2), ("pe", 32), ("w2", 256), ("walpha", 256)]:
    COLS[_name] = NPAR
    NPAR += _n
CCOLS = {}
NCON = 0
for _name, _n in [("ident", P), ("rot", P), ("blk", P), ("cos", S), ("sin", S), ("ccos", 32), ("csin", 32),
                  ("sel", NH * P)]:
    CCOLS[_name] = NCON
    NCON += _n
f32, f32r, bf16, u8 = mybir.dt.float32, mybir.dt.float32r, mybir.dt.bfloat16, mybir.dt.uint8
ACT = mybir.ActivationFunctionType
ALU = mybir.AluOpType
AX = mybir.AxisListType


def widths(name):
    return WIDTHS.get(name[:2], (KD * P, KD * P))


def build(nc, t, out):
    ctx = ExitStack()
    with ctx:
        top = [nc.sbuf_base + 31 & ~31]

        def size(shape, dt):
            n = {bf16: 2, u8: 1}.get(dt, 4)
            for d in shape[1:]:
                n *= d
            return n + (-n % 32)

        def place(name, shape, dt=f32, at=None):
            if at is None:
                at = top[0]
                top[0] += size(shape, dt)
            return nc.alloc_sbuf_tensor_at(name, shape, dt, offset=at)

        x = place("x", [P, KD, S])
        hhi = place("hhi", [P, KD, S], f32r)
        hlo = place("hlo", [P, KD, S], f32r)
        u_at = top[0]
        uhi = place("uhi", [P, KF, S], f32r)
        ulo = place("ulo", [P, KF, S], f32r)
        raw = place("raw", [P, 2, W_SLOT])
        whi = place("whi", [P, 2, W_SLOT // 2], f32r)
        wlo = place("wlo", [P, 2, W_SLOT // 2], f32r)
        cur = place("cur", [P, NPAR])
        con = place("con", [P, NCON])
        conb = place("conb", [P, 3 * P + NB * NCMP + 4], bf16)
        masks = place("masks", [P, 8, P], u8)
        ones = place("ones", [P, P])
        onesm = place("onesm", [P, P])
        eps = place("eps", [P, 2])
        tmp_at = top[0]
        tmp = place("tmp", [P, 6, S])
        at = [u_at]

        def over(name, shape, dt=f32):
            a = at[0]
            at[0] += size(shape, dt)
            assert at[0] <= u_at + 2 * size([P, KF, S], f32), name
            return place(name, shape, dt, a)

        z = over("z", [P, GT_TILES, S])
        y = over("y", [P, KD, S])
        ohi = over("ohi", [P, 4, S], f32r)
        olo = over("olo", [P, 4, S], f32r)
        scratch_at = at[0]
        small = over("small", [P, S])
        nsa_at = at[0]
        vsw = over("vsw", [P, 2, NB, P])
        gt = over("gt", [P, NB, 32])
        gx = over("gx", [P, 4, 2 * NCMP])
        gl = over("gl", [P, 4, 2 * NCMP])
        kcr = over("kcr", [P, 32])
        vcr = over("vcr", [32, P])
        pc = over("pc", [P, NB, NCMP])
        pct = over("pct", [32, S])
        st4 = over("st4", [P, 4, NB])
        st2 = over("st2", [P, 2, 4, 2])
        p_at = at[0]
        pr = over("pr", [P, 2, 2, S])
        prt = over("prt", [P, 2, 2, S])
        xhi = place("xhi", [P, 2, 16, 2 * NCMP], f32r, p_at)
        xlo = place("xlo", [P, 2, 16, 2 * NCMP], f32r, p_at + size([P, 2, 16, 2 * NCMP], f32r))
        zde = place("zde", [P, 2, 2, S // 2], f32, tmp_at)
        ee = place("ee", [P, 2, 2, S // 2], f32, tmp_at + 8 * S)
        xf = place("xf", [P, 16, 2, NCMP], f32, tmp_at + 16 * S)
        at[0] = nsa_at
        rows = over("rows", [NH, 3, S])
        rt = over("rt", [P, NB, NH])
        vm = over("vm", [P, NH, NB, P])
        dm = over("dm", [P, NB, S])
        at[0] = nsa_at
        bcum = over("bcum", [P, 2, S])
        vg = over("vg", [P, NH, NB, P])
        ao = over("ao", [P, 2, 3, 3 * P])
        ad = over("ad", [P, 2, NB, P])
        yhi = place("yhi", [P, KD, S], f32r, scratch_at)
        ylo = place("ylo", [P, KD, S], f32r, scratch_at + size([P, KD, S], f32r))
        assert scratch_at + 2 * size([P, KD, S], f32) <= u_at + 2 * size([P, KF, S], f32)
        bank = [ctx.enter_context(nc.psum_tensor(f"bank{i}", [P, S], f32)) for i in range(8)]

        def cc(name, n=P):
            return con[:, CCOLS[name]:CCOLS[name] + n]

        def par(name, i=0, n=1):
            return cur[:, bass.ds(COLS[name] + i, n)]

        ident, rot, blk, cos, sin = cc("ident"), cc("rot"), cc("blk"), cc("cos", S), cc("sin", S)
        identb, mask_ij, mask_ji = conb[:, 0:P], conb[:, P:2 * P], conb[:, 2 * P:3 * P]
        mask_cmp = conb[:, 3 * P:3 * P + NB * NCMP].rearrange("p (i c) -> p i c", i=NB)

        per_layer = {
            "raw_ready": 16 * UNITS // 2, "hi_done": 2 * UNITS, "lo_done": 2 * UNITS, "tile_done": 2 * UNITS, "unit_free": UNITS,
            "sq_ready": 3 * KD, "ss_ready": 3 * KD, "sd_ready": 3, "rstd_ready": 3, "hf_ready": 3 * KD,
            "hhi_ready": 3 * KD, "hlo_ready": 3 * KD, "silu_ready": 2 * KF, "uhi_ready": 2 * KF, "ulo_ready": 2 * KF,
            "par_ready": 16, "gate_ready": 3 * KD, "y_part": 2 * KD, "y_ready": 3 * KD, "yhi_ready": KD, "ylo_ready": KD,
            "small_ready": 1, "zde_ready": 2, "ee_ready": 16 * 8, "xf_ready": 8, "xhi_ready": 2, "xlo_ready": 2,
            "gx_ready": 4, "gl_ready": 4, "kc_mm": 1, "vc_mm": 1, "kc_ready": 1, "vc_ready": 1,
            "nr_sq": 7, "nr_ss": 7, "nr_sd": 7, "nr_rs": 7, "nr_xn": 7, "nr_rot": 7, "nr_parts": 14, "nr_out": 7,
            "vt_mm": 2, "vt_ready": 2, "gt_mm": 1, "gt_ready": 1,
            "cs_mm": 8, "cs_sub": 8, "cs_exp": 8, "cs_out": 8, "cs_t": 8, "cs_pt": 8,
            "s_mm": 64, "s_max": 64, "s_exp": 64, "s_p": 64, "s_t": 64, "s_pt": 64, "pv": 32,
            "o_hi": 12, "o_lo": 12,
            "row_abs": 1, "row_e": 1, "row_l": 1, "row_m": 1, "rt_mm": 1, "rt_ready": 1,
            "cv": 16, "cv_silu": 4, "og_ready": 4, "vm_mm": 4, "vm_ready": 4,
            "mb_mm": 4, "md_mm": 4, "mm_mm": 4, "d_exp": 4, "em_exp": 4, "sm_mm": 12, "sd_mul": 16, "num_mm": 4, "den_mm": 4,
            "h_out": 4, "ml_free": 4,
            "al_mm": 2, "al_abs": 2, "al_e": 2, "al_l": 2, "al_b": 2, "vg_mm": 4, "vg_ready": 4, "sr_ready": 4, "ad_zero": 1,
            "lv_d": 18, "lv_e": 18, "lv_m": 18, "lv_mm": 20, "lv_rect": 8, "lv_out": 32,
            "og_mm": 4, "og_sq": 4, "og_ss": 4, "og_sd": 4, "og_t": 4,
            "dve_step": DVE_STEPS,
        }
        credit = {"lo_done": 4, "tile_done": 2, "unit_free": 2}

        def semaphore(name):
            return ctx.enter_context(nc.semaphore(name))

        sem = {k: semaphore(k) for k in [*per_layer, "x_in", "con_in", "x_out", "const_set", "held"] if k != "raw_ready"}
        raw_ready = [semaphore("raw_ready0"), semaphore("raw_ready1")]

        class Counts:

            def __init__(self, lay):
                self.lay, self.seen = lay, {}

            def at(self, name, n):
                return per_layer[name] * self.lay + n + credit.get(name, 0)

            def next(self, name, k=1):
                self.seen[name] = self.seen.get(name, 0) + k
                return self.at(name, self.seen[name])

        block = ctx.enter_context(nc.Block())

        @block.sync
        def _(sp):
            sp.dma_start(x[:], t["xT"].rearrange("(k p) t -> p k t", p=P)).then_inc(sem["x_in"], 16)
            sp.dma_start(con[:], t["con"]).then_inc(sem["con_in"], 16)
            sp.dma_start(conb[:], t["conb"]).then_inc(sem["con_in"], 16)
            sp.dma_start(tmp[:, 2:4].rearrange("p a (b c) -> p (a b) c", c=P), t["masks"]).then_inc(sem["con_in"], 16)
            with sp.Fori(0, L) as lay:
                me = Counts(lay)
                for name, n in SECTIONS:
                    w = t[name]
                    wide = w.shape[-1]
                    with sp.Fori(0, n // 2) as i:
                        for j in range(2):
                            sp.wait_ge(sem["lo_done"], me.at("lo_done", 2 * (FIRST[name] + j) - 2 + 4 * i))
                            sp.sem_inc(sem["held"], 1)
                            sp.dma_start(raw[:, j, 0:wide], w[lay, 2 * i + j]).then_inc(raw_ready[j], 16)
            sp.wait_ge(sem["unit_free"], L * UNITS + credit["unit_free"])
            sp.dma_start(out.rearrange("(k p) t -> p k t", p=P), x[:]).then_inc(sem["x_out"], 16)
            sp.wait_ge(sem["x_out"], 16)

        @block.gpsimd
        def _(pool):
            pool.memset(ones[:], 1.0).then_inc(sem["const_set"], 1)
            pool.memset(onesm[:], 1.0 / DM).then_inc(sem["const_set"], 1)
            pool.memset(eps[:, 0:1], EPS).then_inc(sem["const_set"], 1)
            pool.memset(eps[:, 1:2], HD * EPS).then_inc(sem["const_set"], 1)
            pool.sem_inc(sem["lo_done"], credit["lo_done"])
            with pool.Fori(0, L) as lay:
                me = Counts(lay)
                for name, n in SECTIONS:
                    wa, wb = widths(name)
                    with pool.Fori(0, n // 2) as i:
                        for j in range(2):
                            for s, (lo, w) in enumerate(((0, wa), (wa, wb))):
                                pool.wait_ge(sem["hi_done"], me.at("hi_done", 2 * (FIRST[name] + j) + s + 1 + 4 * i))
                                pool.tensor_tensor(wlo[:, s, 0:w], raw[:, j, lo:lo + w],
                                                   whi[:, s, 0:w].bitcast(f32), ALU.subtract).then_inc(sem["lo_done"], 1)

        @block.scalar
        def _(act):
            act.wait_ge(sem["const_set"], 4)
            act.wait_ge(sem["x_in"], 16)
            with act.Fori(0, L) as lay:
                me = Counts(lay)
                A = act.activation

                def split_unit(j, T, r, wa, wb):
                    for s, (lo, w) in enumerate(((0, wa), (wa, wb))):
                        if s == 0:
                            act.wait_ge(raw_ready[j], me.at("raw_ready", r))
                        act.wait_ge(sem["tile_done"], me.at("tile_done", T + s - 1))
                        A(whi[:, s, 0:w], raw[:, j, lo:lo + w], ACT.Copy).then_inc(sem["hi_done"], 1)

                def section(name, extra=None):
                    n = dict(SECTIONS)[name]
                    with act.Fori(0, n // 2) as i:
                        for j in range(2):
                            u0 = FIRST[name] + j
                            split_unit(j, 2 * u0 + 4 * i, 8 * (u0 - j) + 16 + 16 * i, *widths(name))
                            if extra:
                                extra(i, j, 2 * u0 + 4 * i)

                def norm(f):
                    act.wait_ge(sem["unit_free"], me.at("unit_free", (0, FIRST["pA"], FIRST["gu1"])[f]))
                    if f == 0:
                        act.sem_inc(sem["held"], 1)
                        act.dma_start(cur[:], t["params"][lay]).then_inc(sem["par_ready"], 16)
                    for k in range(KD):
                        if k >= 2:
                            act.wait_ge(sem["ss_ready"], me.at("ss_ready", f * KD + k - 1))
                        A(tmp[:, k % 2], x[:, k], ACT.Square).then_inc(sem["sq_ready"], 1)
                    act.wait_ge(sem["ss_ready"], me.at("ss_ready", (f + 1) * KD))
                    A(tmp[:, 5], bank[4][:], ACT.Sqrt, bias=eps[:, 0:1]).then_inc(sem["sd_ready"], 1)
                    for k in range(KD):
                        act.wait_ge(sem["hf_ready"], me.at("hf_ready", f * KD + k + 1))
                        A(hhi[:, k], tmp[:, 2 + k % 2], ACT.Copy).then_inc(sem["hhi_ready"], 1)

                def silu(i, j, T):
                    act.wait_ge(sem["tile_done"], me.at("tile_done", T + 1))
                    A(tmp[:, j], bank[2 * j][:], ACT.Silu).then_inc(sem["silu_ready"], 1)

                norm(0)
                section("gu0", silu)
                section("dn0")
                norm(1)
                section("pA")
                act.wait_ge(sem["zde_ready"], me.next("zde_ready", 2))
                act.wait_ge(sem["con_in"], 48)
                for kv in range(2):
                    for par2 in range(2):
                        for g in range(2):
                            act.dma_start(ee[par2 * HD:(par2 + 1) * HD, kv, g], zde[g * HD:(g + 1) * HD, kv, par2]
                                          ).then_inc(sem["ee_ready"], 16)
                for kv in range(2):
                    act.wait_ge(sem["xf_ready"], me.next("xf_ready", 4))
                    A(xhi[:, kv], xf[:].rearrange("p l g c -> p l (g c)"), ACT.Copy).then_inc(sem["xhi_ready"], 1)
                for kv in range(2):
                    for ht in range(2):
                        u = FIRST["cmp"] + 2 * kv + ht
                        split_unit(ht, 2 * u, 8 * (u - ht) + 16, KD * P, KD * P)
                act.wait_ge(sem["gx_ready"], me.next("gx_ready", 4))
                A(gl[:], gx[:], ACT.Gelu_apprx_tanh).then_inc(sem["gl_ready"], 4)

                def norm_rope(src, n, scale, e):
                    A(tmp[:, 0, 0:n], src, ACT.Square).then_inc(sem["nr_sq"], 1)
                    act.wait_ge(sem["nr_ss"], me.next("nr_ss"))
                    A(tmp[:, 1, 0:n], bank[4][:, 0:n], ACT.Sqrt, scale=scale, bias=eps[:, e:e + 1]).then_inc(sem["nr_sd"], 1)

                act.wait_ge(sem["xlo_ready"], me.next("xlo_ready", 2))
                for i, (c, e) in enumerate([(KS, 0), (KW, 0)] + [(Q + i, 1) for i in range(4)]):
                    if i:
                        act.wait_ge(sem["nr_rs"], me.next("nr_rs"))
                    norm_rope(z[:, c], S, float(HD) if e else 1.0, e)
                act.wait_ge(sem["nr_rs"], me.next("nr_rs"))
                act.wait_ge(sem["kc_ready"], me.next("kc_ready"))
                norm_rope(kcr[:, 0:NCMP], NCMP, 1.0, 0)
                for i in range(2):
                    act.wait_ge(sem["vt_mm"], me.next("vt_mm"))
                    A(vsw[:, i], bank[6 + i][:].rearrange("p (a b) -> p a b", a=NB), ACT.Copy).then_inc(sem["vt_ready"], 1)
                act.wait_ge(sem["gt_mm"], me.next("gt_mm"))
                A(gt[:], bank[6][:, 0:NB * 32].rearrange("p (a b) -> p a b", a=NB), ACT.Sigmoid).then_inc(sem["gt_ready"], 1)
                for b in range(8):
                    act.wait_ge(sem["cs_sub"], me.next("cs_sub"))
                    A(pc[:], pc[:], ACT.Exp).then_inc(sem["cs_exp"], 1)
                    act.wait_ge(sem["cs_t"], me.next("cs_t"))
                    if b:
                        act.wait_ge(sem["pv"], me.at("pv", 4 * b))
                    A(pct[0:NCMP, :], bank[6][0:NCMP, :], ACT.Copy).then_inc(sem["cs_pt"], 1)

                    def exps(it):
                        n = (it + 1) * P
                        for w in range(2):
                            act.wait_ge(sem["s_max"], me.next("s_max"))
                            A(pr[:, it % 2, w, 0:n], bank[4 + w][:, 0:n], ACT.Exp, bias=st2[:, it % 2, 0, w:w + 1],
                                      accum_out=st2[:, it % 2, 1, w:w + 1]).then_inc(sem["s_exp"], 1)

                    exps(0)
                    for it in range(NB):
                        n = (it + 1) * P
                        for w in range(2):
                            act.wait_ge(sem["s_t"], me.next("s_t"))
                            A(prt[:, it % 2, w, 0:n], bank[6][:, 0:n], ACT.Copy).then_inc(sem["s_pt"], 1)
                            if it + 1 < NB and w == 1:
                                exps(it + 1)
                section("pB")

                def gate(i, j, T, b):
                    act.wait_ge(sem["tile_done"], me.at("tile_done", T + 1))
                    A(tmp[:, j], bank[2 * j][:], ACT.Sigmoid, bias=par("gbias", 2 * i + j + b * KD)
                      ).then_inc(sem["gate_ready"], 1)

                act.wait_ge(sem["o_lo"], me.at("o_lo", 4))
                act.sem_inc(sem["held"], 1)
                section("cb0", lambda i, j, T: gate(i, j, T, 0))
                act.wait_ge(sem["row_abs"], me.next("row_abs"))
                A(tmp[0:NH, 1], tmp[0:NH, 0], ACT.Exp, scale=-1.0).then_inc(sem["row_e"], 1)
                act.wait_ge(sem["row_e"], me.at("row_e", 1))
                A(tmp[0:NH, 2], tmp[0:NH, 1], ACT.Ln, bias=ones[0:NH, 0:1]).then_inc(sem["row_l"], 1)
                for c in range(4):
                    act.wait_ge(sem["cv"], me.next("cv", 4))
                    A(z[:, c], tmp[:, 3 + c % 2], ACT.Silu).then_inc(sem["cv_silu"], 1)
                for h in range(NH):
                    A(z[:, 8 + h], z[:, 8 + h], ACT.Sigmoid).then_inc(sem["og_ready"], 1)
                for h in range(NH):
                    act.wait_ge(sem["vm_mm"], me.next("vm_mm"))
                    A(vm[:, h], bank[6 + h % 2][:].rearrange("p (a b) -> p a b", a=NB), ACT.Copy).then_inc(sem["vm_ready"], 1)
                act.wait_ge(sem["rt_ready"], me.next("rt_ready"))
                for h in range(NH):
                    if h:
                        act.wait_ge(sem["num_mm"], me.at("num_mm", h))
                        act.wait_ge(sem["den_mm"], me.at("den_mm", h))
                    act.wait_ge(sem["mb_mm"], me.next("mb_mm"))
                    for jt in range(NB - 1):
                        A(dm[:, jt, (jt + 1) * P:S], bank[4][:, (jt + 1) * P:S], ACT.Exp, scale=-1.0, bias=rt[:, jt, h:h + 1])
                    act.wait_ge(sem["md_mm"], me.next("md_mm"))
                    for jt in range(NB):
                        i = A(dm[:, jt, jt * P:(jt + 1) * P], bank[5][:, jt * P:(jt + 1) * P], ACT.Exp, scale=-1.0,
                              bias=rt[:, jt, h:h + 1])
                    i.then_inc(sem["d_exp"], 1)
                    act.wait_ge(sem["mm_mm"], me.next("mm_mm"))
                    if h:
                        act.wait_ge(sem["h_out"], me.at("h_out", h))
                    A(tmp[:, 5], bank[6][:], ACT.Exp, scale=-1.0).then_inc(sem["em_exp"], 1)
                section("pC")
                act.wait_ge(sem["o_lo"], me.at("o_lo", 8))
                act.sem_inc(sem["held"], 1)
                section("cb1", lambda i, j, T: gate(i, j, T, 1))
                for p in range(2):
                    act.wait_ge(sem["al_abs"], me.next("al_abs"))
                    A(tmp[:, 2], tmp[:, 1], ACT.Exp, scale=-1.0).then_inc(sem["al_e"], 1)
                    act.wait_ge(sem["al_e"], me.at("al_e", p + 1))
                    A(tmp[:, 3], tmp[:, 2], ACT.Ln, bias=ones[:, 0:1]).then_inc(sem["al_l"], 1)
                for h in range(NH):
                    A(z[:, 8 + h], z[:, 8 + h], ACT.Silu).then_inc(sem["sr_ready"], 1)
                for h in range(NH):
                    act.wait_ge(sem["vg_mm"], me.next("vg_mm"))
                    A(vg[:, h], bank[6 + h % 2][:].rearrange("p (a b) -> p a b", a=NB), ACT.Copy).then_inc(sem["vg_ready"], 1)
                for p in range(2):
                    for v, s in enumerate(LEVELS):
                        act.wait_ge(sem["lv_d"], me.next("lv_d"))
                        if (p, v) != (0, 0):
                            act.wait_ge(sem["lv_m"], me.at("lv_m", 9 * p + v))
                        A(tmp[:, 1], tmp[:, 0], ACT.Exp, scale=1.0 / 16).then_inc(sem["lv_e"], 1)
                        if s >= P:
                            act.wait_ge(sem["lv_mm"], me.at("lv_mm", 10 * p + v + 1))
                            if p and s == 2 * P:
                                act.wait_ge(sem["og_mm"], me.at("og_mm", 2))
                            for hh in range(2):
                                b = bank[4 + 2 * (v % 2) + hh]
                                if s == 2 * P:
                                    A(ao[:, hh, 0, P:3 * P], b[:, 0:2 * P], ACT.Copy)
                                    i = A(ao[:, hh, 1, 0:2 * P], b[:, 2 * P:4 * P], ACT.Copy)
                                else:
                                    A(ao[:, hh, 0, 0:P], b[:, 0:P], ACT.Copy)
                                    i = A(ao[:, hh, 2, 0:P], b[:, P:2 * P], ACT.Copy)
                                i.then_inc(sem["lv_rect"], 1)
                    for hh in range(2):
                        act.wait_ge(sem["og_mm"], me.next("og_mm"))
                        A(tmp[:, 2], bank[4 + hh][:], ACT.Square).then_inc(sem["og_sq"], 1)
                        act.wait_ge(sem["og_ss"], me.next("og_ss"))
                        if p or hh:
                            act.wait_ge(sem["og_t"], me.at("og_t", 2 * p + hh))
                        A(tmp[:, 3], bank[6][:], ACT.Sqrt, scale=float(KD), bias=eps[:, 0:1]).then_inc(sem["og_sd"], 1)
                act.wait_ge(sem["o_lo"], me.at("o_lo", 12))
                act.sem_inc(sem["held"], 1)
                section("cb2", lambda i, j, T: gate(i, j, T, 2))
                act.wait_ge(sem["y_ready"], me.at("y_ready", 3 * KD))
                for k in range(KD):
                    A(yhi[:, k], y[:, k], ACT.Copy).then_inc(sem["yhi_ready"], 1)
                section("wo")
                norm(2)
                section("gu1", silu)
                section("dn1")

        @block.vector
        def _(dve):
            dve.sem_inc(sem["unit_free"], credit["unit_free"])
            dve.wait_ge(sem["con_in"], 48)
            dve.wait_ge(sem["const_set"], 4)
            dve.tensor_copy(masks[:], tmp[:, 2:4].rearrange("p a (b c) -> p (a b) c", c=P)).then_inc(sem["held"], 1)
            with dve.Fori(0, L) as lay:
                me = Counts(lay)

                def norm(f):
                    if f == 0:
                        dve.wait_ge(sem["par_ready"], me.at("par_ready", 16))
                    dve.wait_ge(sem["sd_ready"], me.at("sd_ready", f + 1))
                    dve.reciprocal(tmp[:, 4], tmp[:, 5]).then_inc(sem["rstd_ready"], 1)
                    dve.wait_ge(sem["rstd_ready"], me.at("rstd_ready", f + 1))
                    for k in range(KD):
                        dve.scalar_tensor_tensor(tmp[:, 2 + k % 2], x[:, k], par("norm", f * KD + k), tmp[:, 4],
                                                 ALU.mult, ALU.mult).then_inc(sem["hf_ready"], 1)
                        dve.wait_ge(sem["hhi_ready"], me.at("hhi_ready", f * KD + k + 1))
                        dve.tensor_tensor(hlo[:, k], tmp[:, 2 + k % 2], hhi[:, k].bitcast(f32), ALU.subtract
                                          ).then_inc(sem["hlo_ready"], 1)
                        dve.wait_ge(sem["hlo_ready"], me.at("hlo_ready", f * KD + k + 1))
                    dve.sem_inc(sem["held"], 1)

                def ffn(f):
                    with dve.Fori(0, KF // 2) as i:
                        for j in range(2):
                            n, m, c = FIRST[f"gu{f}"] + j + 2 * i, f * KF + j + 2 * i, 2 * i + j
                            dve.wait_ge(sem["silu_ready"], me.at("silu_ready", m + 1))
                            dve.wait_ge(sem["tile_done"], me.at("tile_done", 2 * n + 2))
                            dve.tensor_tensor(tmp[:, 2 + j], tmp[:, j], bank[2 * j + 1][:], ALU.mult
                                              ).then_inc(sem["unit_free"], 1)
                            dve.wait_ge(sem["unit_free"], me.at("unit_free", n + 1))
                            dve.tensor_copy(uhi[:, c], tmp[:, 2 + j]).then_inc(sem["uhi_ready"], 1)
                            dve.wait_ge(sem["uhi_ready"], me.at("uhi_ready", m + 1))
                            dve.tensor_tensor(ulo[:, c], tmp[:, 2 + j], uhi[:, c].bitcast(f32), ALU.subtract
                                              ).then_inc(sem["ulo_ready"], 1)
                    with dve.Fori(0, KD // 2) as i:
                        for j in range(2):
                            n, c = FIRST[f"dn{f}"] + j + 2 * i, 2 * i + j
                            dve.wait_ge(sem["tile_done"], me.at("tile_done", 2 * n + 2))
                            dve.scalar_tensor_tensor(x[:, c], bank[2 * j][:], 0.5, x[:, c], ALU.mult, ALU.add
                                                     ).then_inc(sem["unit_free"], 1)
                    dve.wait_ge(sem["unit_free"], me.at("unit_free", FIRST[f"dn{f}"] + KD))
                    dve.sem_inc(sem["held"], 1)

                def project(name, group):
                    with dve.Fori(0, 3) as i:
                        for j in range(2):
                            u, c = FIRST[name] + j + 2 * i, 4 * i + 2 * j
                            dve.wait_ge(sem["tile_done"], me.at("tile_done", 2 * u + 1))
                            dve.tensor_scalar(z[:, c], bank[2 * j][:], par("bias", c + group * GT_TILES), None, ALU.add)
                            dve.wait_ge(sem["tile_done"], me.at("tile_done", 2 * u + 2))
                            dve.tensor_scalar(z[:, c + 1], bank[2 * j + 1][:], par("bias", c + 1 + group * GT_TILES),
                                              None, ALU.add).then_inc(sem["unit_free"], 1)
                    dve.wait_ge(sem["unit_free"], me.at("unit_free", FIRST[name] + 6))
                    dve.sem_inc(sem["held"], 1)

                def combine(b):
                    with dve.Fori(0, KD // 2) as i:
                        for j in range(2):
                            u, c = FIRST[f"cb{b}"] + j + 2 * i, 2 * i + j
                            dve.wait_ge(sem["gate_ready"], me.at("gate_ready", b * KD + c + 1))
                            dve.wait_ge(sem["tile_done"], me.at("tile_done", 2 * u + 2))
                            dve.tensor_tensor(tmp[:, 2 + j] if b else y[:, c], tmp[:, j], bank[2 * j + 1][:], ALU.mult
                                              ).then_inc(sem["unit_free"], 1)
                            dve.wait_ge(sem["unit_free"], me.at("unit_free", u + 1))
                            if b:
                                dve.tensor_tensor(y[:, c], y[:, c], tmp[:, 2 + j], ALU.add
                                                  ).then_inc(sem["y_ready"], 1)
                            else:
                                dve.sem_inc(sem["y_ready"], 1)
                    dve.wait_ge(sem["y_ready"], me.at("y_ready", (b + 1) * KD))
                    dve.sem_inc(sem["held"], 1)

                def out_parts(o, src):
                    dve.tensor_copy(ohi[:, o % 4], src).then_inc(sem["o_hi"], 1)
                    dve.wait_ge(sem["o_hi"], me.next("o_hi"))
                    dve.tensor_tensor(olo[:, o % 4], src, ohi[:, o % 4].bitcast(f32), ALU.subtract).then_inc(sem["o_lo"], 1)

                norm(0)
                ffn(0)
                norm(1)
                project("pA", 0)
                dve.tensor_copy(small[:], z[:, SM]).then_inc(sem["small_ready"], 1)
                for kv in range(2):
                    dve.tensor_copy(zde[:, kv], z[:, KC + kv].rearrange("p (m a) -> p a m", a=2)).then_inc(sem["zde_ready"], 1)
                dve.wait_ge(sem["ee_ready"], me.at("ee_ready", 128))
                for kv in range(2):
                    if kv:
                        dve.wait_ge(sem["xlo_ready"], me.at("xlo_ready", kv))
                    for g in range(2):
                        for half in range(2):
                            src = ee[:, kv, g].rearrange("p (c l) -> p l c", l=8)[:, :, half:half + NCMP]
                            pe_ = par("pe", 16 * kv + 8 * half, 8).unsqueeze(2).broadcast_to([P, 8, NCMP])
                            dve.tensor_tensor(xf[:, 8 * half:8 * half + 8, g], src, pe_, ALU.add).then_inc(sem["xf_ready"], 1)
                    dve.wait_ge(sem["xhi_ready"], me.next("xhi_ready"))
                    dve.wait_ge(sem["xf_ready"], me.at("xf_ready", 4 * kv + 4))
                    dve.tensor_tensor(xlo[:, kv], xf[:].rearrange("p l g c -> p l (g c)"), xhi[:, kv].bitcast(f32),
                                              ALU.subtract).then_inc(sem["xlo_ready"], 1)
                    dve.wait_ge(sem["xlo_ready"], me.next("xlo_ready"))
                for kv in range(2):
                    for ht in range(2):
                        u = FIRST["cmp"] + 2 * kv + ht
                        dve.wait_ge(sem["tile_done"], me.at("tile_done", 2 * u + 2))
                        dve.tensor_copy(gx[:, 2 * kv + ht], bank[2 * ht][:, 0:2 * NCMP]).then_inc(sem["unit_free"], 1)
                dve.wait_ge(sem["unit_free"], me.at("unit_free", FIRST["pB"]))
                dve.sem_inc(sem["gx_ready"], 4)

                def norm_rope(src, n, gain, dst, co, si):
                    dve.wait_ge(sem["nr_sd"], me.next("nr_sd"))
                    dve.reciprocal(tmp[:, 2, 0:n], tmp[:, 1, 0:n]).then_inc(sem["nr_rs"], 1)
                    dve.wait_ge(sem["nr_rs"], me.next("nr_rs"))
                    dve.scalar_tensor_tensor(tmp[:, 3, 0:n], src, par("qkn", gain), tmp[:, 2, 0:n],
                                                     ALU.mult, ALU.mult).then_inc(sem["nr_xn"], 1)
                    dve.wait_ge(sem["nr_xn"], me.next("nr_xn"))
                    dve.tensor_tensor(tmp[:, 5, 0:n], tmp[:, 3, 0:n], co, ALU.mult).then_inc(sem["nr_parts"], 1)
                    dve.wait_ge(sem["nr_rot"], me.next("nr_rot"))
                    dve.tensor_tensor(tmp[:, 4, 0:n], bank[5][:, 0:n], si, ALU.mult).then_inc(sem["nr_parts"], 1)
                    dve.wait_ge(sem["nr_parts"], me.next("nr_parts", 2))
                    dve.tensor_tensor(dst, tmp[:, 4, 0:n], tmp[:, 5, 0:n], ALU.add).then_inc(sem["nr_out"], 1)
                    dve.wait_ge(sem["nr_out"], me.next("nr_out"))

                for c, g in [(KS, 2), (KW, 3)] + [(Q + i, 0) for i in range(4)]:
                    norm_rope(z[:, c], S, g, z[:, c], cos, sin)
                dve.wait_ge(sem["vc_mm"], me.next("vc_mm"))
                dve.tensor_copy(vcr[0:NCMP, :], bank[7][0:NCMP, 0:P]).then_inc(sem["vc_ready"], 1)
                dve.wait_ge(sem["kc_mm"], me.next("kc_mm"))
                dve.tensor_copy(kcr[:, 0:NCMP], bank[5][:, 0:NCMP]).then_inc(sem["kc_ready"], 1)
                dve.wait_ge(sem["kc_ready"], me.next("kc_ready"))
                norm_rope(kcr[:, 0:NCMP], NCMP, 1, kcr[:, 0:NCMP], cc("ccos", NCMP), cc("csin", NCMP))
                dve.wait_ge(sem["gt_ready"], me.at("gt_ready", 1))
                for b in range(8):
                    tt, g = b // 2, b % 2
                    head = tt + 4 * g
                    dve.wait_ge(sem["cs_mm"], me.next("cs_mm"))
                    cs = bank[6][:, 0:NB * 32].rearrange("p (i c) -> p i c", c=32)[:, :, 0:NCMP]
                    dve.tensor_reduce(st4[:, 0], cs, AX.X, ALU.max).then_inc(sem["dve_step"], 1)
                    dve.wait_ge(sem["dve_step"], me.next("dve_step"))
                    dve.tensor_scalar(st4[:, 1], st4[:, 0], -1e20, None, ALU.max).then_inc(sem["dve_step"], 1)
                    dve.wait_ge(sem["dve_step"], me.next("dve_step"))
                    dve.tensor_tensor(pc[:], cs, st4[:, 1].unsqueeze(2).broadcast_to([P, NB, NCMP]), ALU.subtract).then_inc(sem["cs_sub"], 1)
                    dve.wait_ge(sem["cs_sub"], me.next("cs_sub"))
                    dve.wait_ge(sem["cs_exp"], me.next("cs_exp"))
                    dve.tensor_reduce(st4[:, 2], pc[:], AX.X, ALU.add).then_inc(sem["dve_step"], 1)
                    dve.wait_ge(sem["dve_step"], me.next("dve_step"))
                    dve.tensor_scalar(st4[:, 2], st4[:, 2], 1e-30, None, ALU.max).then_inc(sem["dve_step"], 1)
                    dve.wait_ge(sem["dve_step"], me.next("dve_step"))
                    dve.reciprocal(st4[:, 3], st4[:, 2]).then_inc(sem["dve_step"], 1)
                    dve.wait_ge(sem["dve_step"], me.next("dve_step"))
                    dve.tensor_tensor(st4[:, 3], st4[:, 3], gt[:, :, 3 * head], ALU.mult).then_inc(sem["dve_step"], 1)
                    dve.wait_ge(sem["dve_step"], me.next("dve_step"))
                    dve.tensor_tensor(pc[:], pc[:], st4[:, 3].unsqueeze(2).broadcast_to([P, NB, NCMP]), ALU.mult).then_inc(sem["cs_out"], 1)
                    dve.wait_ge(sem["cs_out"], me.next("cs_out"))

                    def maxima(it):
                        n = (it + 1) * P
                        for w in range(2):
                            dve.wait_ge(sem["s_mm"], me.next("s_mm"))
                            dve.tensor_reduce(st2[:, it % 2, 0, w:w + 1], bank[4 + w][:, 0:n], AX.X, ALU.max,
                                                      negate=True).then_inc(sem["s_max"], 1)

                    maxima(0)
                    for it in range(NB):
                        n = (it + 1) * P
                        dve.wait_ge(sem["s_exp"], me.next("s_exp", 2))
                        dve.reciprocal(st2[:, it % 2, 2], st2[:, it % 2, 1]).then_inc(sem["dve_step"], 1)
                        dve.wait_ge(sem["dve_step"], me.next("dve_step"))
                        dve.tensor_tensor(st2[:, it % 2, 3], st2[:, it % 2, 2],
                                                  gt[:, it, 3 * head + 1:3 * head + 3], ALU.mult).then_inc(sem["dve_step"], 1)
                        dve.wait_ge(sem["dve_step"], me.next("dve_step"))
                        for w in range(2):
                            dve.tensor_scalar(pr[:, it % 2, w, 0:n], pr[:, it % 2, w, 0:n],
                                                      st2[:, it % 2, 3, w:w + 1], None, ALU.mult).then_inc(sem["s_p"], 1)
                        if it + 1 < NB:
                            maxima(it + 1)
                    if g:
                        dve.wait_ge(sem["pv"], me.at("pv", 8 * tt + 8))
                        out_parts(tt, bank[7][:])
                project("pB", 1)
                combine(0)
                dve.scalar_tensor_tensor(tmp[0:NH, 0], small[R_F:R_F + NH], -1.0, small[R_F:R_F + NH], ALU.mult, ALU.max).then_inc(sem["row_abs"], 1)
                dve.tensor_copy(tmp[0:NH, 4], small[R_I:R_I + NH]).then_inc(sem["dve_step"], 1)
                dve.wait_ge(sem["dve_step"], me.next("dve_step"))
                dve.wait_ge(sem["row_l"], me.next("row_l"))
                dve.scalar_tensor_tensor(tmp[0:NH, 3], small[R_F:R_F + NH], 0.0, tmp[0:NH, 2], ALU.min, ALU.subtract).then_inc(sem["dve_step"], 1)
                dve.wait_ge(sem["dve_step"], me.next("dve_step"))
                one = ones[0:NH, 0:1].broadcast_to([NH, S])
                dve.tensor_tensor_scan(tmp[0:NH, 5], one, tmp[0:NH, 3], 0.0, ALU.mult, ALU.add).then_inc(sem["dve_step"], 1)
                dve.wait_ge(sem["dve_step"], me.next("dve_step"))
                dve.tensor_tensor(rows[:, 0], tmp[0:NH, 4], tmp[0:NH, 5], ALU.subtract).then_inc(sem["dve_step"], 1)
                dve.wait_ge(sem["dve_step"], me.next("dve_step"))
                dve.tensor_tensor_scan(rows[:, 1], one, rows[:, 0], 0.0, ALU.mult, ALU.max).then_inc(sem["dve_step"], 1)
                dve.wait_ge(sem["dve_step"], me.next("dve_step"))
                dve.tensor_tensor(rows[:, 2], tmp[0:NH, 5], rows[:, 1], ALU.add).then_inc(sem["row_m"], 1)
                dve.wait_ge(sem["row_m"], me.next("row_m"))
                for c in range(4):
                    acc = tmp[:, 3 + c % 2]
                    if c >= 2:
                        dve.wait_ge(sem["cv_silu"], me.at("cv_silu", c - 1))
                    dve.tensor_scalar(acc, z[:, c], par("convw", 4 * c + 3), par("convb", c), ALU.mult, ALU.add).then_inc(sem["cv"], 1)
                    dve.wait_ge(sem["cv"], me.next("cv"))
                    for d in (1, 2, 3):
                        dve.scalar_tensor_tensor(acc[:, d:S], z[:, c, 0:S - d], par("convw", 4 * c + 3 - d),
                                                         acc[:, d:S], ALU.mult, ALU.add).then_inc(sem["cv"], 1)
                        dve.wait_ge(sem["cv"], me.next("cv"))
                dve.wait_ge(sem["rt_mm"], me.next("rt_mm"))
                dve.tensor_copy(rt[:].rearrange("p a b -> p (a b)"), bank[4][:, 0:NB * NH]).then_inc(sem["rt_ready"], 1)
                for h in range(NH):
                    dve.wait_ge(sem["d_exp"], me.next("d_exp"))
                    for jt in range(NB):
                        if jt < 3:
                            dve.wait_ge(sem["sm_mm"], me.next("sm_mm"))
                        src = (bank[7][:, 0:S], bank[6][:, 0:3 * P], bank[4][:, 0:2 * P], bank[4][:, 2 * P:3 * P])[jt]
                        dve.scalar_tensor_tensor(dm[:, jt, jt * P:S], src, HD ** -0.5, dm[:, jt, jt * P:S],
                                                         ALU.mult, ALU.mult).then_inc(sem["sd_mul"], 1)
                    dve.wait_ge(sem["den_mm"], me.next("den_mm"))
                    dve.wait_ge(sem["em_exp"], me.next("em_exp"))
                    dve.scalar_tensor_tensor(tmp[:, 1], bank[6][:], -1.0, tmp[:, 5], ALU.mult, ALU.max).then_inc(sem["dve_step"], 1)
                    dve.wait_ge(sem["dve_step"], me.next("dve_step"))
                    dve.tensor_tensor(tmp[:, 0], bank[6][:], tmp[:, 1], ALU.max).then_inc(sem["dve_step"], 1)
                    dve.wait_ge(sem["dve_step"], me.next("dve_step"))
                    dve.reciprocal(tmp[:, 1], tmp[:, 0]).then_inc(sem["dve_step"], 1)
                    dve.wait_ge(sem["dve_step"], me.next("dve_step"))
                    dve.wait_ge(sem["num_mm"], me.next("num_mm"))
                    dve.tensor_tensor(tmp[:, 2], bank[5][:], tmp[:, 1], ALU.mult).then_inc(sem["h_out"], 1)
                    dve.wait_ge(sem["h_out"], me.next("h_out"))
                    dve.wait_ge(sem["og_ready"], me.at("og_ready", h + 1))
                    dve.tensor_tensor(tmp[:, 3], tmp[:, 2], z[:, 8 + h], ALU.mult).then_inc(sem["dve_step"], 1)
                    dve.wait_ge(sem["dve_step"], me.next("dve_step"))
                    if h == 0:
                        dve.wait_ge(sem["gate_ready"], me.at("gate_ready", KD))
                        dve.wait_ge(sem["tile_done"], me.at("tile_done", 2 * FIRST["pC"]))
                    out_parts(4 + h, tmp[:, 3])
                dve.wait_ge(sem["o_lo"], me.at("o_lo", 8))
                dve.sem_inc(sem["held"], 1)
                project("pC", 2)
                combine(1)
                for p in range(2):
                    dve.wait_ge(sem["al_mm"], me.next("al_mm"))
                    dve.tensor_scalar(tmp[:, 0], bank[4][:], par("balpha", p), None, ALU.add).then_inc(sem["dve_step"], 1)
                    dve.wait_ge(sem["dve_step"], me.next("dve_step"))
                    dve.scalar_tensor_tensor(tmp[:, 1], tmp[:, 0], -1.0, tmp[:, 0], ALU.mult, ALU.max).then_inc(sem["al_abs"], 1)
                    dve.wait_ge(sem["al_abs"], me.next("al_abs"))
                    dve.wait_ge(sem["al_l"], me.next("al_l"))
                    dve.scalar_tensor_tensor(tmp[:, 4], tmp[:, 0], 0.0, tmp[:, 3], ALU.min, ALU.subtract).then_inc(sem["dve_step"], 1)
                    dve.wait_ge(sem["dve_step"], me.next("dve_step"))
                    dve.tensor_tensor_scan(bcum[:, p], ones[:, 0:1].broadcast_to([P, S]), tmp[:, 4], 0.0,
                                                   ALU.mult, ALU.add).then_inc(sem["al_b"], 1)
                    dve.wait_ge(sem["al_b"], me.next("al_b"))
                    dve.tensor_scalar(z[:, p], z[:, p], HD ** -0.5, None, ALU.mult).then_inc(sem["dve_step"], 1)
                    dve.wait_ge(sem["dve_step"], me.next("dve_step"))
                dve.memset(ad[:], 0.0).then_inc(sem["ad_zero"], 1)
                dve.wait_ge(sem["ad_zero"], me.next("ad_zero"))
                for p in range(2):
                    def emit(v, s):
                        dve.wait_ge(sem["lv_mm"], me.at("lv_mm", 10 * p + v + 1))
                        if p and v == 2:
                            dve.wait_ge(sem["og_mm"], me.at("og_mm", 2))
                        for hh in range(2):
                            m = masks[:, v - 2].unsqueeze(1).broadcast_to([P, NB, P])
                            data = bank[4 + 2 * (v % 2) + hh][:].rearrange("p (a b) -> p a b", a=NB)
                            dve.sem_inc(sem["held"], 1)
                            dve.copy_predicated(ad[:, hh], m, data).then_inc(sem["lv_out"], 1)
                            dve.wait_ge(sem["lv_out"], me.next("lv_out"))

                    for v, s in enumerate(LEVELS):
                        B = bcum[:, p].rearrange("p (n h s) -> p n h s", h=2, s=s)
                        D = tmp[:, 0].rearrange("p (n h s) -> p n h s", h=2, s=s)
                        E = tmp[:, 1].rearrange("p (n h s) -> p n h s", h=2, s=s)
                        M = tmp[:, 2 + v % 2].rearrange("p (n h s) -> p n h s", h=2, s=s)
                        q = z[:, p].rearrange("p (n h s) -> p n h s", h=2, s=s)
                        k = z[:, 2 + p].rearrange("p (n h s) -> p n h s", h=2, s=s)
                        nb = S // (2 * s)
                        mid = B[:, :, 0, s - 1:s].broadcast_to([P, nb, s])
                        if (p, v) != (0, 0):
                            dve.wait_ge(sem["lv_e"], me.at("lv_e", 9 * p + v))
                        dve.tensor_tensor(D[:, :, 0], mid, B[:, :, 0], ALU.subtract).then_inc(sem["dve_step"], 1)
                        dve.wait_ge(sem["dve_step"], me.next("dve_step"))
                        dve.tensor_tensor(D[:, :, 1], B[:, :, 1], mid, ALU.subtract).then_inc(sem["lv_d"], 1)
                        dve.wait_ge(sem["lv_e"], me.next("lv_e"))
                        if v >= 2:
                            dve.wait_ge(sem["lv_mm"], me.at("lv_mm", 10 * p + v - 1))
                        elif p and v == 0:
                            dve.wait_ge(sem["og_t"], me.at("og_t", 2))
                        dve.tensor_tensor(M[:, :, 0], E[:, :, 0], k[:, :, 0], ALU.mult).then_inc(sem["dve_step"], 1)
                        dve.wait_ge(sem["dve_step"], me.next("dve_step"))
                        dve.tensor_tensor(M[:, :, 1], E[:, :, 1], q[:, :, 1], ALU.mult).then_inc(sem["lv_m"], 1)
                        dve.wait_ge(sem["lv_m"], me.next("lv_m"))
                        if v >= 3:
                            emit(v - 1, LEVELS[v - 1])
                    emit(8, 1)
                    emit(9, 0)
                    for hh in range(2):
                        h = 2 * p + hh
                        dve.wait_ge(sem["og_sd"], me.next("og_sd"))
                        dve.reciprocal(tmp[:, 4], tmp[:, 3]).then_inc(sem["dve_step"], 1)
                        dve.wait_ge(sem["dve_step"], me.next("dve_step"))
                        dve.scalar_tensor_tensor(tmp[:, 5], bank[4 + hh][:], par("gn"), tmp[:, 4], ALU.mult, ALU.mult).then_inc(sem["og_t"], 1)
                        dve.wait_ge(sem["og_t"], me.next("og_t"))
                        dve.wait_ge(sem["sr_ready"], me.at("sr_ready", h + 1))
                        dve.tensor_tensor(tmp[:, 5], tmp[:, 5], z[:, 8 + h], ALU.mult).then_inc(sem["dve_step"], 1)
                        dve.wait_ge(sem["dve_step"], me.next("dve_step"))
                        if h == 0:
                            dve.wait_ge(sem["tile_done"], me.at("tile_done", 2 * FIRST["cb2"]))
                        out_parts(8 + h, tmp[:, 5])
                        dve.wait_ge(sem["o_lo"], me.at("o_lo", 8 + h + 1))
                dve.sem_inc(sem["held"], 1)
                combine(2)
                for k in range(KD):
                    dve.wait_ge(sem["yhi_ready"], me.at("yhi_ready", k + 1))
                    dve.tensor_tensor(ylo[:, k], y[:, k], yhi[:, k].bitcast(f32), ALU.subtract).then_inc(sem["ylo_ready"], 1)
                dve.wait_ge(sem["ylo_ready"], me.at("ylo_ready", KD))
                dve.sem_inc(sem["held"], 1)
                with dve.Fori(0, 2) as i:
                    for j in range(2):
                        u, c = FIRST["wo"] + j + 2 * i, 4 * i + 2 * j
                        dve.wait_ge(sem["tile_done"], me.at("tile_done", 2 * u + 1))
                        dve.tensor_tensor(x[:, c], bank[2 * j][:], x[:, c], ALU.add)
                        dve.wait_ge(sem["tile_done"], me.at("tile_done", 2 * u + 2))
                        dve.tensor_tensor(x[:, c + 1], bank[2 * j + 1][:], x[:, c + 1], ALU.add).then_inc(sem["unit_free"], 1)
                dve.wait_ge(sem["unit_free"], me.at("unit_free", FIRST["gu1"]))
                dve.sem_inc(sem["held"], 1)
                norm(2)
                ffn(1)

        @block.tensor
        def _(pe):
            mm = pe.matmul
            pe.sem_inc(sem["tile_done"], credit["tile_done"])
            pe.wait_ge(sem["const_set"], 4)
            pe.wait_ge(sem["con_in"], 48)
            with pe.Fori(0, L) as lay:
                me = Counts(lay)

                def tile(T, s, outp, parts, free=None, start=True, stop=True):
                    pe.wait_ge(sem["lo_done"], me.at("lo_done", T + s + 1))
                    if free is not None:
                        pe.wait_ge(sem["unit_free"], me.at("unit_free", free))
                    for k, (mhi, mlo) in enumerate(parts):
                        wh, wl = whi[:, s, k * P:(k + 1) * P], wlo[:, s, k * P:(k + 1) * P]
                        mm(outp, wh, mhi, start=start and k == 0, stop=False)
                        mm(outp, wh, mlo, start=False, stop=False)
                        last = mm(outp, wl, mhi, start=False, stop=stop and k == len(parts) - 1)
                    last.then_inc(sem["tile_done"], 1)

                def section(name, a, b, one=False):
                    with pe.Fori(0, dict(SECTIONS)[name] // 2) as i:
                        for j in range(2):
                            u = FIRST[name] + j + 2 * i
                            tile(2 * u, 0, bank[2 * j][:], a, free=u - 1, stop=not one)
                            tile(2 * u, 1, bank[2 * j + (not one)][:], b, start=not one)

                hp = [(hhi[:, k], hlo[:, k]) for k in range(KD)]
                up = [(uhi[:, k], ulo[:, k]) for k in range(KF)]
                op = [(ohi[:, k], olo[:, k]) for k in range(4)]
                yp = [(yhi[:, k], ylo[:, k]) for k in range(KD)]

                def norm(f):
                    for k in range(KD):
                        pe.wait_ge(sem["sq_ready"], me.at("sq_ready", f * KD + k + 1))
                        mm(bank[4][:], onesm[:], tmp[:, k % 2], start=k == 0, stop=k == KD - 1
                           ).then_inc(sem["ss_ready"], 1)
                    pe.wait_ge(sem["hlo_ready"], me.at("hlo_ready", (f + 1) * KD))
                    pe.sem_inc(sem["held"], 1)

                def ffn(f):
                    section(f"gu{f}", hp, hp)
                    pe.wait_ge(sem["ulo_ready"], me.at("ulo_ready", (f + 1) * KF))
                    pe.sem_inc(sem["held"], 1)
                    section(f"dn{f}", up[:KF // 2], up[KF // 2:], one=True)

                def transposes(dst, src):
                    for a in range(NB):
                        i = pe.transpose(dst[:, a * P:(a + 1) * P], src[:, a * P:(a + 1) * P], ident)
                    return i

                norm(0)
                ffn(0)
                norm(1)
                section("pA", hp, hp)
                pe.wait_ge(sem["xlo_ready"], me.next("xlo_ready", 2))
                for kv in range(2):
                    for ht in range(2):
                        u = FIRST["cmp"] + 2 * kv + ht
                        for s in range(2):
                            tile(2 * u, s, bank[2 * ht][:, 0:2 * NCMP], [(xhi[:, kv, 8 * s + l], xlo[:, kv, 8 * s + l])
                                                                        for l in range(8)],
                                 free=u - 1 if s == 0 else None, start=s == 0, stop=s == 1)
                for i in range(6):
                    pe.wait_ge(sem["nr_sq"], me.next("nr_sq"))
                    if i:
                        pe.wait_ge(sem["nr_sd"], me.next("nr_sd"))
                    mm(bank[4][:], blk, tmp[:, 0], start=True, stop=True).then_inc(sem["nr_ss"], 1)
                    pe.wait_ge(sem["nr_xn"], me.next("nr_xn"))
                    if i:
                        pe.wait_ge(sem["nr_out"], me.next("nr_out"))
                    mm(bank[5][:], rot, tmp[:, 3], start=True, stop=True).then_inc(sem["nr_rot"], 1)
                pe.wait_ge(sem["nr_out"], me.next("nr_out"))
                pe.wait_ge(sem["nr_sd"], me.next("nr_sd"))
                pe.wait_ge(sem["gl_ready"], me.next("gl_ready", 4))
                for g in range(2):
                    for ht in range(2):
                        i = mm(bank[5][g * HD:(g + 1) * HD, 0:NCMP], par("w2", ht * HD, HD),
                               gl[:, ht, g * NCMP:(g + 1) * NCMP], start=ht == 0, stop=ht == 1)
                i.then_inc(sem["kc_mm"], 1)
                for g in range(2):
                    for ht in range(2):
                        i = mm(bank[7][0:NCMP, g * HD:(g + 1) * HD], gl[:, 2 + ht, g * NCMP:(g + 1) * NCMP],
                               par("w2", 128 + ht * HD, HD), start=ht == 0, stop=ht == 1)
                i.then_inc(sem["vc_mm"], 1)
                pe.wait_ge(sem["nr_sq"], me.next("nr_sq"))
                mm(bank[4][:, 0:NCMP], blk, tmp[:, 0, 0:NCMP], start=True, stop=True).then_inc(sem["nr_ss"], 1)
                pe.wait_ge(sem["nr_xn"], me.next("nr_xn"))
                mm(bank[5][:, 0:NCMP], rot, tmp[:, 3, 0:NCMP], start=True, stop=True).then_inc(sem["nr_rot"], 1)
                pe.wait_ge(sem["nr_out"], me.next("nr_out"))
                pe.wait_ge(sem["vc_ready"], me.next("vc_ready"))
                transposes(bank[6], z[:, VS]).then_inc(sem["vt_mm"], 1)
                transposes(bank[7], z[:, VW]).then_inc(sem["vt_mm"], 1)
                pe.wait_ge(sem["vt_ready"], me.next("vt_ready", 2))
                pe.sem_inc(sem["held"], 1)
                for a in range(NB):
                    i = pe.transpose(bank[6][:, a * 32:(a + 1) * 32], small[R_G:R_G + 32, a * P:(a + 1) * P],
                                     ident[R_G:R_G + 32, R_G:R_G + 32])
                i.then_inc(sem["gt_mm"], 1)
                pe.wait_ge(sem["gt_ready"], me.next("gt_ready"))
                for b in range(8):
                    tt, g = b // 2, b % 2
                    r = slice(g * HD, (g + 1) * HD)

                    def scores(it, w):
                        if it:
                            pe.wait_ge(sem["s_exp"], me.at("s_exp", 8 * b + 2 * it - 1 + w))
                        elif b:
                            pe.wait_ge(sem["s_exp"], me.at("s_exp", 8 * b - 1 + w))
                        mm(bank[4 + w][:, 0:(it + 1) * P], z[r, Q + tt, it * P:(it + 1) * P], z[r, KS + w, 0:(it + 1) * P],
                           start=True, stop=False)
                        mm(bank[4 + w][:, it * P:(it + 1) * P], identb, mask_ij, start=False, stop=True).then_inc(sem["s_mm"], 1)

                    if b:
                        pe.wait_ge(sem["s_pt"], me.at("s_pt", 8 * b))
                    for it in range(NB):
                        mm(bank[6][:, it * 32:it * 32 + NCMP], z[r, Q + tt, it * P:(it + 1) * P], kcr[r, 0:NCMP],
                           start=True, stop=False)
                        i = mm(bank[6][:, it * 32:it * 32 + NCMP], identb, mask_cmp[:, it], start=False, stop=True)
                    i.then_inc(sem["cs_mm"], 1)
                    scores(0, 0)
                    scores(0, 1)
                    pe.wait_ge(sem["cs_out"], me.next("cs_out"))
                    for it in range(NB):
                        i = pe.transpose(bank[6][0:NCMP, it * P:(it + 1) * P], pc[:, it], ident)
                    i.then_inc(sem["cs_t"], 1)
                    pe.wait_ge(sem["cs_pt"], me.next("cs_pt"))
                    for it in range(NB):
                        for w in range(2):
                            pe.wait_ge(sem["s_p"], me.next("s_p"))
                            if it or w:
                                pe.wait_ge(sem["s_pt"], me.at("s_pt", 8 * b + 2 * it + w))
                            for jt in range(it + 1):
                                i = pe.transpose(bank[6][:, jt * P:(jt + 1) * P], pr[:, it % 2, w, jt * P:(jt + 1) * P], ident)
                            i.then_inc(sem["s_t"], 1)
                            if it + 1 < NB:
                                scores(it + 1, w)
                        if g == 0 and it == 0 and tt:
                            pe.wait_ge(sem["o_lo"], me.at("o_lo", tt))
                        pe.wait_ge(sem["s_pt"], me.at("s_pt", 8 * b + 2 * it + 2))
                        o = bank[7][r, it * P:(it + 1) * P]
                        for w in range(2):
                            for jt in range(it + 1):
                                mm(o, vsw[:, w, jt, r], prt[:, it % 2, w, jt * P:(jt + 1) * P], start=w + jt == 0, stop=False)
                        mm(o, vcr[0:NCMP, r], pct[0:NCMP, it * P:(it + 1) * P], start=False, stop=True).then_inc(sem["pv"], 1)
                section("pB", hp, hp)
                pe.wait_ge(sem["o_lo"], me.at("o_lo", 4))
                pe.sem_inc(sem["held"], 1)
                section("cb0", hp, op)
                pe.wait_ge(sem["row_m"], me.next("row_m"))
                pe.sem_inc(sem["held"], 1)
                for a in range(NB):
                    i = pe.transpose(bank[4][:, a * NH:(a + 1) * NH], rows[0:NH, 0, a * P:(a + 1) * P], ident[0:NH, 0:NH])
                i.then_inc(sem["rt_mm"], 1)
                for h in range(NH):
                    if h >= 2:
                        pe.wait_ge(sem["vm_ready"], me.at("vm_ready", h - 1))
                    transposes(bank[6 + h % 2], z[:, 4 + h]).then_inc(sem["vm_mm"], 1)
                pe.wait_ge(sem["vm_ready"], me.at("vm_ready", 4))
                pe.wait_ge(sem["rt_ready"], me.at("rt_ready", 1))
                pe.wait_ge(sem["cv_silu"], me.at("cv_silu", 4))
                sel = lambda h: con[0:NH, CCOLS["sel"] + h * P:CCOLS["sel"] + (h + 1) * P]
                for h in range(NH):
                    r = slice((h % 2) * HD, (h % 2 + 1) * HD)
                    if h:
                        pe.wait_ge(sem["h_out"], me.at("h_out", h))
                    mm(bank[4][:], sel(h), rows[0:NH, 1], start=True, stop=True).then_inc(sem["mb_mm"], 1)
                    mm(bank[5][:], sel(h), rows[0:NH, 1], start=True, stop=False)
                    mm(bank[5][:], identb, mask_ji.unsqueeze(1).broadcast_to([P, NB, P]), start=False, stop=True).then_inc(sem["md_mm"], 1)
                    mm(bank[6][:], sel(h), rows[0:NH, 2], start=True, stop=True).then_inc(sem["mm_mm"], 1)
                    q, k = z[r, h // 2], z[r, 2 + h // 2]
                    mm(bank[7][:], k[:, 0:P], q, start=True, stop=True).then_inc(sem["sm_mm"], 1)
                    pe.wait_ge(sem["d_exp"], me.next("d_exp"))
                    pe.wait_ge(sem["em_exp"], me.next("em_exp"))
                    mm(bank[6][:, 0:3 * P], k[:, P:2 * P], q[:, P:S], start=True, stop=True).then_inc(sem["sm_mm"], 1)
                    mm(bank[4][:, 0:2 * P], k[:, 2 * P:3 * P], q[:, 2 * P:S], start=True, stop=True)
                    mm(bank[4][:, 2 * P:3 * P], k[:, 3 * P:S], q[:, 3 * P:S], start=True, stop=True).then_inc(sem["sm_mm"], 1)
                    for lhs, b in ((None, 5), (ones, 6)):
                        for jt in range(NB):
                            if b == 5:
                                pe.wait_ge(sem["sd_mul"], me.next("sd_mul"))
                            i = mm(bank[b][:, jt * P:S], lhs[:] if lhs is not None else vm[:, h, jt], dm[:, jt, jt * P:S],
                                   start=jt == 0, stop=jt == NB - 1)
                        i.then_inc(sem["num_mm"] if b == 5 else sem["den_mm"], 1)
                pe.wait_ge(sem["o_lo"], me.at("o_lo", 8))
                pe.sem_inc(sem["held"], 1)
                section("pC", hp, hp)
                section("cb1", hp, op)
                for p in range(2):
                    if p:
                        pe.wait_ge(sem["al_abs"], me.at("al_abs", p))
                    mm(bank[4][:], cur[R_LR:R_LR + 16, COLS["walpha"] + p * P:COLS["walpha"] + (p + 1) * P],
                               small[R_LR:R_LR + 16], start=True, stop=True).then_inc(sem["al_mm"], 1)
                for h in range(NH):
                    if h >= 2:
                        pe.wait_ge(sem["vg_ready"], me.at("vg_ready", h - 1))
                    transposes(bank[6 + h % 2], z[:, 4 + h]).then_inc(sem["vg_mm"], 1)
                pe.wait_ge(sem["vg_ready"], me.at("vg_ready", 4))
                pe.wait_ge(sem["al_b"], me.at("al_b", 2))
                pe.wait_ge(sem["ad_zero"], me.at("ad_zero", 1))
                for p in range(2):
                    for v in range(len(LEVELS) + 1):
                        s = LEVELS[v] if v < len(LEVELS) else 0
                        if s:
                            pe.wait_ge(sem["lv_m"], me.next("lv_m"))
                        if v in (2, 3):
                            pe.wait_ge(sem["lv_rect"], me.at("lv_rect", 4 * p + 2 * (v - 1)))
                        elif v >= 4:
                            pe.wait_ge(sem["lv_out"], me.at("lv_out", 16 * p + 2 * (v - 3)))
                        elif p:
                            pe.wait_ge(sem["og_t"], me.at("og_t", 2))
                        for hh in range(2):
                            r = slice(hh * HD, (hh + 1) * HD)
                            b = bank[4 + 2 * (v % 2) + hh]
                            M = tmp[r, 2 + v % 2]
                            a, c = (M, M) if s else (z[r, 2 + p], z[r, p])
                            if s == 2 * P:
                                for jt in range(2):
                                    i = mm(b[:, jt * 2 * P:(jt + 1) * 2 * P], a[:, jt * P:(jt + 1) * P], c[:, 2 * P:S],
                                           start=True, stop=True)
                            elif s == P:
                                for jt in range(2):
                                    i = mm(b[:, jt * P:(jt + 1) * P], a[:, 2 * jt * P:(2 * jt + 1) * P],
                                           c[:, (2 * jt + 1) * P:(2 * jt + 2) * P], start=True, stop=True)
                            else:
                                for jt in range(NB):
                                    i = mm(b[:, jt * P:(jt + 1) * P], a[:, jt * P:(jt + 1) * P], c[:, jt * P:(jt + 1) * P],
                                           start=True, stop=True)
                        i.then_inc(sem["lv_mm"], 1)
                    for hh in range(2):
                        h = 2 * p + hh
                        if hh == 0:
                            pe.wait_ge(sem["lv_out"], me.at("lv_out", 16 * (p + 1)))
                            pe.wait_ge(sem["lv_rect"], me.at("lv_rect", 4 * (p + 1)))
                        for jt in range(NB):
                            o = bank[4 + hh][:]
                            i = mm(o[:, jt * P:(jt + 1) * P], vg[:, h, jt], ad[:, hh, jt], start=jt == 0, stop=jt == NB - 1)
                            if jt < NB - 1:
                                mm(o[:, (jt + 1) * P:S], vg[:, h, jt], ao[:, hh, jt, 0:S - (jt + 1) * P], start=False, stop=False)
                        i.then_inc(sem["og_mm"], 1)
                    for hh in range(2):
                        pe.wait_ge(sem["og_sq"], me.next("og_sq"))
                        if hh:
                            pe.wait_ge(sem["og_sd"], me.at("og_sd", 2 * p + hh))
                        mm(bank[6][:], onesm[:], tmp[:, 2], start=True, stop=True).then_inc(sem["og_ss"], 1)
                pe.wait_ge(sem["o_lo"], me.at("o_lo", 12))
                pe.sem_inc(sem["held"], 1)
                section("cb2", hp, op)
                pe.wait_ge(sem["ylo_ready"], me.at("ylo_ready", KD))
                pe.sem_inc(sem["held"], 1)
                section("wo", yp, yp)
                norm(2)
                ffn(1)


def kernel(**a):
    import numpy as np
    import ml_dtypes
    import concourse.bacc as _bacc
    from concourse.bass_utils import run_bass_kernel_spmd as _run
    a = {k: np.asarray(v) for k, v in a.items()}

    def tiles(w):
        l, k, m = w.shape
        return w.reshape(l, k // P, P, m // P, P).transpose(0, 3, 2, 1, 4).reshape(l, m // P, P, k)

    def pairs(w):
        l, n, p, k = w.shape
        return w.reshape(l, n // 2, 2, p, k).transpose(0, 1, 3, 2, 4).reshape(l, n // 2, p, 2 * k)

    arr = {"xT": np.ascontiguousarray(a["x"][0].T)}
    for f in (0, 1):
        g, u = tiles(a[f"ffn{f + 1}_w_gate"]), tiles(a[f"ffn{f + 1}_w_up"])
        arr[f"gu{f}"] = np.concatenate([g, u], 3)
        arr[f"dn{f}"] = tiles(a[f"ffn{f + 1}_w_down"])
    sizes = [256, 256, 512, 512, 16, 512] + [128] * 6 + [24, 512, 512, 512, 4, 4, DM, DM, DM]
    off = np.concatenate([[0], np.cumsum(sizes)])
    names = ["aq", "ak", "av", "ar", "alr", "bq", "bkc", "bvc", "bks", "bvs", "bkw", "bvw", "bg", "cqk", "cv", "co",
             "ci", "cf", "ga", "gb", "gc"]
    at = {n: np.arange(off[i], off[i + 1]) for i, n in enumerate(names)}
    small = np.full(P, -1)
    small[R_F:R_F + 4], small[R_I:R_I + 4], small[R_LR:R_LR + 16], small[R_G:R_G + 24] = at["cf"], at["ci"], at["alr"], at["bg"]
    pair = np.concatenate([np.concatenate([np.arange(h * HD, (h + 1) * HD), np.arange((h + 4) * HD, (h + 5) * HD)])
                           for h in range(4)])
    order = {"pA": [small, at["bkc"], at["bvc"], at["bq"][pair], at["bks"], at["bkw"], at["bvs"], at["bvw"], np.full(P, -1)],
             "pB": [at["cqk"], at["cv"], at["co"]], "pC": [at["aq"], at["ak"], at["av"], at["ar"]]}
    w_in = np.concatenate([a["w_in"], np.zeros((L, DM, 1), np.float32)], 2)
    b_in = np.concatenate([a["b_in"], np.zeros((L, 1), np.float32)], 1)
    cols = lambda v: v.reshape(v.shape[0], -1, P).transpose(0, 2, 1)
    bias = []
    for name, idx in order.items():
        idx = np.concatenate(idx)
        arr[name] = pairs(tiles(w_in[:, :, idx]))
        bias.append(cols(b_in[:, idx]))
    w1 = a["nsa_cmp_w1"].reshape(L, 2, 16, P, 2, P).transpose(0, 1, 4, 3, 2, 5)
    arr["cmp"] = w1.reshape(L, 4, P, 16 * P)
    branch = [a["w_branch"][:, 1][:, pair], a["w_branch"][:, 2], a["w_branch"][:, 0]]
    gates = [at["gb"], at["gc"], at["ga"]]
    for b in range(3):
        arr[f"cb{b}"] = np.concatenate([tiles(a["w_in"][:, :, gates[b]]), tiles(branch[b])], 3)
    arr["wo"] = pairs(tiles(a["w_out"]))
    walpha = np.zeros((L, P, 256), np.float32)
    walpha[:, R_LR:R_LR + 16] = a["gla_w_alpha"]
    params = [cols(a["ffn1_norm"]), cols(a["mix_norm"]), cols(a["ffn2_norm"]), *bias, *[cols(a["b_in"][:, g]) for g in gates],
              a["mlstm_conv_w"].reshape(L, 4, 4, P).transpose(0, 3, 2, 1).reshape(L, P, 16), cols(a["mlstm_conv_b"]),
              np.concatenate([a["nsa_qk_norm"]] * 2, 2).transpose(0, 2, 1), a["gla_out_norm"][:, :, None], cols(a["gla_b_alpha"]),
              a["nsa_cmp_pos"].reshape(L, 2, 16, P).transpose(0, 3, 1, 2).reshape(L, P, 32),
              a["nsa_cmp_w2"].reshape(L, 2, 2, P, HD).transpose(0, 3, 1, 2, 4).reshape(L, P, 256), walpha]
    arr["params"] = np.concatenate(params, 2)
    half = HD // 2
    freqs = np.float32(10000.0) ** (-np.arange(half, dtype=np.float32) / np.float32(half))
    fr = np.tile(freqs, 4)[:, None].astype(np.float32)
    ang = fr * np.arange(S, dtype=np.float32)[None]
    cang = fr * (np.arange(32, dtype=np.float32)[None] * CS + 2 * CS - 1)
    rot = np.zeros((P, P), np.float32)
    for q in range(0, P, HD):
        for i in range(half):
            rot[q + half + i, q + i] = -1.0
            rot[q + i, q + half + i] = 1.0
    r = np.arange(P)
    blk = (r[:, None] // HD == r[None] // HD) / np.float32(HD)
    sel = np.zeros((P, NH * P), np.float32)
    for h in range(NH):
        sel[h, h * P:(h + 1) * P] = 1.0
    arr["con"] = np.concatenate([np.eye(P), rot, blk, np.cos(ang), np.sin(ang), np.cos(cang), np.sin(cang), sel], 1).astype(np.float32)
    later = np.where(r[None] > r[:, None], -1e30, 0.0)
    tok = np.arange(S).reshape(NB, P).T
    cend = np.arange(NCMP) * CS + 2 * CS - 1
    cm = np.where(cend[None, None] > tok[:, :, None], -1e30, 0.0).reshape(P, -1)
    arr["conb"] = np.concatenate([np.eye(P), later, -later.T, cm, np.zeros((P, 4))], 1).astype(ml_dtypes.bfloat16)
    j, i = r[:, None], r[None]
    lv = [(j // (2 * s) == i // (2 * s)) & (j % (2 * s) < s) & (i % (2 * s) >= s) for s in LEVELS[2:]] + [j == i]
    arr["masks"] = np.stack(lv, 1).astype(np.float32)
    arr = {k: np.ascontiguousarray(v) for k, v in arr.items()}
    nc = _bacc.Bacc("TRN2", target_bir_lowering=False, num_devices=1)
    t = {k: nc.dram_tensor(k, v.shape, mybir.dt.from_np(v.dtype), kind="ExternalInput").ap() for k, v in arr.items()}
    o = nc.dram_tensor("outT", (DM, S), f32, kind="ExternalOutput").ap()
    build(nc, t, o)
    got = _run(nc, [arr], core_ids=[0])
    return np.ascontiguousarray(got.results[0]["outT"].T)[None]
```

```python
import concourse.bass as bass
from concourse import mybir
from contextlib import ExitStack

P = 128
L, S, DM, FF = 2, 512, 1024, 2816
KD, KF, NB = DM // P, FF // P, S // P
HD = 64
NCMP, CS = S // 16 - 1, 16
NH, NPAIR = 4, 4
GT_TILES = 12
MT_TILES = 24
W_SLOT = KF * P
EPS = 1e-6
DVE_STEPS = 139
LEVELS = [256, 128, 64, 32, 16, 8, 4, 2, 1]
SM, VS, VW, KC, VC, Q, KS, KW = 0, 1, 2, 3, 4, 5, 9, 10
R_F, R_I, R_LR, R_G = 0, 32, 64, 96
SECTIONS = [("gu0", KF), ("dn0", KD), ("pA", 6), ("pM0", 2), ("cq", 8), ("pM1", 6), ("cb0", KD), ("cb1", KD),
            ("cb2", KD), ("wo", KD // 2), ("gu1", KF), ("dn1", KD)]
FIRST = {}
UNITS = 0
for _name, _n in SECTIONS:
    FIRST[_name] = UNITS
    UNITS += _n
WIDTHS = {"gu": (KD * P, KD * P), "dn": (KF // 2 * P, KF // 2 * P), "cb": (KD * P, 4 * P)}
PM1 = ([4 * n if n < 4 else 16 + (n - 4) * 80 // 64 for n in range(69)], [KD * (i + 1) for i in range(12)])
CB = ([4 * n for n in range(25)], [12 * (i // 2) + (12 if i % 2 else 8) for i in range(2 * KD)])
COLS = {}
NPAR = 0
for _name, _n in [("norm", 3 * KD), ("bias", GT_TILES + MT_TILES), ("gbias", 3 * KD), ("convw", 16), ("convb", 4),
                  ("qkn", 4), ("gn", 1), ("balpha", 2), ("pe", 32), ("w2", 256), ("walpha", 256)]:
    COLS[_name] = NPAR
    NPAR += _n
CCOLS = {}
NCON = 0
for _name, _n in [("ident", P), ("rot", P), ("blk", P), ("cos", S), ("sin", S), ("ccos", 32), ("csin", 32),
                  ("sel", NH * P)]:
    CCOLS[_name] = NCON
    NCON += _n
f32, f32r, bf16, u8 = mybir.dt.float32, mybir.dt.float32r, mybir.dt.bfloat16, mybir.dt.uint8
ACT = mybir.ActivationFunctionType
ALU = mybir.AluOpType
AX = mybir.AxisListType


def ended(plan, n):
    at, ends = plan
    return [i for i, e in enumerate(ends) if n and at[n - 1] < e <= at[n]]


def widths(name):
    return WIDTHS.get(name[:2], (KD * P, KD * P))


def build(nc, t, out):
    ctx = ExitStack()
    with ctx:
        top = [nc.sbuf_base + 31 & ~31]

        def size(shape, dt):
            n = {bf16: 2, u8: 1}.get(dt, 4)
            for d in shape[1:]:
                n *= d
            return n + (-n % 32)

        def place(name, shape, dt=f32, at=None):
            if at is None:
                at = top[0]
                top[0] += size(shape, dt)
            return nc.alloc_sbuf_tensor_at(name, shape, dt, offset=at)

        x = place("x", [P, KD, S])
        hhi = place("hhi", [P, KD, S], f32r)
        hlo = place("hlo", [P, KD, S], f32r)
        u_at = top[0]
        uhi = place("uhi", [P, KF, S], f32r)
        ulo = place("ulo", [P, KF, S], f32r)
        raw = place("raw", [P, 2, W_SLOT])
        whi = place("whi", [P, 2, W_SLOT // 2], f32r)
        wlo = place("wlo", [P, 2, W_SLOT // 2], f32r)
        cur = place("cur", [P, NPAR])
        con = place("con", [P, NCON])
        conb = place("conb", [P, 3 * P + NB * NCMP + 4], bf16)
        masks = place("masks", [P, 8, P], u8)
        ones = place("ones", [P, P])
        onesm = place("onesm", [P, P])
        eps = place("eps", [P, 2])
        tmp_at = top[0]
        tmp = place("tmp", [P, 6, S])
        def within(name, tile, shape, dt=f32, skip=0):
            assert tile * 4 * S + skip + size(shape, dt) <= 2 * size([P, KF, S], f32), name
            return place(name, shape, dt, u_at + tile * 4 * S + skip)

        Z0, M0 = 0, GT_TILES - 1
        z = within("z", Z0, [P, GT_TILES, S])
        zm = within("zm", M0, [P, MT_TILES, S])
        ohi = within("ohi", M0 + MT_TILES, [P, 4, S], f32r)
        olo = within("olo", M0 + MT_TILES + 4, [P, 4, S], f32r)
        last = M0 + MT_TILES + 8
        small = z[:, SM]
        y = within("y", KC, [P, KD, S])
        xhi = within("xhi", M0 + 12, [P, 2, 16, 2 * NCMP], f32r)
        xlo = within("xlo", M0 + 16, [P, 2, 16, 2 * NCMP], f32r)
        glr = within("glr", M0 + 20, [P, 2, 2, 4, 32])
        gx = within("gx", M0 + 21, [P, 4, 2 * NCMP])
        gl = within("gl", M0 + 21, [P, 4, 2 * NCMP], skip=1024)
        pc = within("pc", M0 + 22, [P, 2, NB * 4, 32])
        prt = within("prt", VS, [P, 2, 2, S])
        pr = tmp[:, 0:4].rearrange("p (a w) c -> p a w c", a=2)
        pct = tmp[:, 4:6]
        zde = tmp[:, 0:2].rearrange("p k (a m) -> p k a m", a=2)
        ee = tmp[:, 2:4].rearrange("p k (g m) -> p k g m", g=2)
        xf = place("xf", [P, 16, 2, NCMP], f32, tmp_at + 16 * S)
        kcr = place("kcr", [P, 32])
        st4 = place("st4", [P, 4, NB * 4])
        st2 = place("st2", [P, 2, 4, 2])
        rt = place("rt", [P, NB, NH])
        tail = [raw[:, w, 2 * KD * P:W_SLOT] for w in range(2)]
        vsw = [tail[w][:, 0:S].rearrange("p (a b) -> p a b", a=NB) for w in range(2)]
        vcr = tail[0][:, S:S + P]
        gt = tail[1][:, S:S + P].rearrange("p (a b) -> p a b", a=NB)
        dm = [tail[0][:, 0:S], tail[1][:, 0:3 * P], tail[1][:, 3 * P:5 * P], tail[0][:, S:S + P]]
        rows = within("rows", VS, [NH, 2, S])
        row0 = within("row0", last, [NH, S])
        bcum = within("bcum", M0, [P, 2, S])
        ge = within("ge", M0 + 2, [P, 2, S])
        ad = within("ad", M0 + 4, [P, 2, NB, P])
        ao = within("ao", M0 + 6, [P, 2, 3, 3 * P])
        yhi = within("yhi", M0, [P, KD, S], f32r)
        ylo = within("ylo", M0 + KD, [P, KD, S], f32r)
        bank = [ctx.enter_context(nc.psum_tensor(f"bank{i}", [P, S], f32)) for i in range(8)]

        def cc(name, n=P):
            return con[:, CCOLS[name]:CCOLS[name] + n]

        def par(name, i=0, n=1):
            return cur[:, bass.ds(COLS[name] + i, n)]

        ident, rot, blk, cos, sin = cc("ident"), cc("rot"), cc("blk"), cc("cos", S), cc("sin", S)
        identb, mask_ij, mask_ji = conb[:, 0:P], conb[:, P:2 * P], conb[:, 2 * P:3 * P]
        mask_cmp = conb[:, 3 * P:3 * P + NB * NCMP].rearrange("p (i c) -> p i c", i=NB)

        per_layer = {
            "raw_ready": 16 * UNITS // 2, "hi_done": 2 * UNITS, "lo_done": 2 * UNITS, "tile_done": 2 * UNITS, "unit_free": UNITS,
            "sq_ready": 3 * KD, "sum_part": 3 * KD, "ss_ready": 3, "ln_ready": 3, "rstd_ready": 3, "hf_ready": 3 * KD,
            "hhi_ready": 3 * KD, "hlo_ready": 3 * KD, "silu_ready": 2 * KF, "uhi_ready": 2 * KF, "ulo_ready": 2 * KF,
            "par_ready": 16, "gate_ready": 3 * KD, "y_ready": 3 * KD, "yhi_ready": KD, "ylo_ready": KD,
            "glr_zero": 1, "zde_ready": 2, "ee_ready": 16 * 8, "xf_ready": 8, "xhi_ready": 2, "xlo_ready": 2,
            "gx_ready": 1, "gl_ready": 1, "glr_ready": 2, "kc_mm": 1, "vc_mm": 1, "kc_ready": 1, "vc_ready": 1,
            "nr_sq": 7, "nr_ss": 7, "nr_ln": 7, "nr_rs": 7, "nr_xn": 7, "nr_rot": 7, "nr_parts": 14, "nr_out": 7,
            "vt_mm": 2, "vt_ready": 2, "gt_mm": 1, "gt_ready": 1,
            "cs_mm": 2, "cs_sub": 2, "cs_exp": 2, "cs_out": 2, "cs_t": 2, "cs_pt": 2,
            "s_mm": 64, "s_max": 64, "s_exp": 64, "s_p": 64, "s_t": 64, "s_pt": 64, "pv": 32,
            "o_hi": 12, "o_lo": 12,
            "row_abs": 1, "row_e": 1, "row_l": 1, "row_m": 1, "rt_mm": 1, "rt_ready": 1,
            "cv": 16, "cv_silu": 4, "og_ready": 4, "vm_mm": 4, "vm_ready": 4,
            "mb_mm": 4, "md_mm": 4, "mm_mm": 4, "d_exp": 4, "em_exp": 4, "sm_mm": 12, "sd_mul": 16, "num_mm": 4, "den_mm": 4,
            "h_out": 4, "h_gated": 4,
            "al_mm": 2, "al_abs": 2, "al_e": 2, "al_l": 2, "al_b": 2, "vg_mm": 4, "vg_ready": 4, "sr_ready": 4, "ad_zero": 1,
            "lv_d": 18, "lv_e": 18, "lv_m": 18, "lv_mm": 20, "lv_rect": 8, "lv_out": 32,
            "og_mm": 4, "og_sq": 4, "og_ss": 4, "og_ln": 4, "og_rs": 4, "og_t": 4, "og_out": 4,
            "dve_step": DVE_STEPS,
        }
        credit = {"lo_done": 4, "tile_done": 2, "unit_free": 2, "sq_ready": KD, "sum_part": KD}

        def semaphore(name):
            return ctx.enter_context(nc.semaphore(name))

        sem = {k: semaphore(k) for k in [*per_layer, "x_in", "con_in", "x_out", "const_set", "masks_set", "held"] if k != "raw_ready"}
        raw_ready = [semaphore("raw_ready0"), semaphore("raw_ready1")]

        class Counts:

            def __init__(self, lay):
                self.lay, self.seen = lay, {}

            def at(self, name, n):
                return per_layer[name] * self.lay + n + credit.get(name, 0)

            def next(self, name, k=1):
                self.seen[name] = self.seen.get(name, 0) + k
                return self.at(name, self.seen[name])

        block = ctx.enter_context(nc.Block())

        @block.sync
        def _(sp):
            sp.dma_start(x[:], t["xT"].rearrange("(k p) t -> p k t", p=P)).then_inc(sem["x_in"], 16)
            sp.dma_start(con[:], t["con"]).then_inc(sem["con_in"], 16)
            sp.dma_start(conb[:], t["conb"]).then_inc(sem["con_in"], 16)
            sp.dma_start(tmp[:, 2:4].rearrange("p a (b c) -> p (a b) c", c=P), t["masks"]).then_inc(sem["con_in"], 16)
            with sp.Fori(0, L) as lay:
                me = Counts(lay)
                for name, n in SECTIONS:
                    w = t[name]
                    wide = w.shape[-1]
                    with sp.Fori(0, n // 2) as i:
                        for j in range(2):
                            sp.wait_ge(sem["lo_done"], me.at("lo_done", 2 * (FIRST[name] + j) - 2 + 4 * i))
                            sp.sem_inc(sem["held"], 1)
                            sp.dma_start(raw[:, j, 0:wide], w[lay, 2 * i + j]).then_inc(raw_ready[j], 16)
            sp.wait_ge(sem["unit_free"], L * UNITS + credit["unit_free"])
            sp.dma_start(out.rearrange("(k p) t -> p k t", p=P), x[:]).then_inc(sem["x_out"], 16)
            sp.wait_ge(sem["x_out"], 16)

        @block.gpsimd
        def _(pool):
            pool.memset(ones[:], 1.0).then_inc(sem["const_set"], 1)
            pool.memset(onesm[:], 1.0 / DM).then_inc(sem["const_set"], 1)
            pool.memset(eps[:, 0:1], EPS).then_inc(sem["const_set"], 1)
            pool.memset(eps[:, 1:2], HD * EPS).then_inc(sem["const_set"], 1)
            pool.sem_inc(sem["lo_done"], credit["lo_done"])
            with pool.Fori(0, L) as lay:
                me = Counts(lay)
                for name, n in SECTIONS:
                    wa, wb = widths(name)
                    with pool.Fori(0, n // 2) as i:
                        for j in range(2):
                            for s, (lo, w) in enumerate(((0, wa), (wa, wb))):
                                pool.wait_ge(sem["hi_done"], me.at("hi_done", 2 * (FIRST[name] + j) + s + 1 + 4 * i))
                                pool.tensor_tensor(wlo[:, s, 0:w], raw[:, j, lo:lo + w],
                                                   whi[:, s, 0:w].bitcast(f32), ALU.subtract).then_inc(sem["lo_done"], 1)

        @block.scalar
        def _(act):
            act.wait_ge(sem["const_set"], 4)
            act.wait_ge(sem["x_in"], 16)
            for c in range(KD):
                if c >= 2:
                    act.wait_ge(sem["sum_part"], c - 1)
                act.activation(tmp[:, c % 2], x[:, c], ACT.Square).then_inc(sem["sq_ready"], 1)
            with act.Fori(0, L) as lay:
                me = Counts(lay)
                A = act.activation

                def split_unit(j, T, r, wa, wb):
                    for s, (lo, w) in enumerate(((0, wa), (wa, wb))):
                        if s == 0:
                            act.wait_ge(raw_ready[j], me.at("raw_ready", r))
                        act.wait_ge(sem["tile_done"], me.at("tile_done", T + s - 1))
                        A(whi[:, s, 0:w], raw[:, j, lo:lo + w], ACT.Copy).then_inc(sem["hi_done"], 1)

                def split_tile(name, T):
                    u, s = FIRST[name] + T // 2, T % 2
                    wa, wb = widths(name)
                    if s == 0:
                        act.wait_ge(raw_ready[u % 2], me.at("raw_ready", 8 * (u - u % 2) + 16))
                    act.wait_ge(sem["tile_done"], me.at("tile_done", 2 * u + s - 1))
                    A(whi[:, s, 0:(wa, wb)[s]], raw[:, u % 2, s * wa:s * wa + (wa, wb)[s]], ACT.Copy).then_inc(sem["hi_done"], 1)

                def section(name, extra=None):
                    def unit(i, j, split=True):
                        u0 = FIRST[name] + j
                        if split:
                            split_unit(j, 2 * u0 + 4 * i, 8 * (u0 - j) + 16 + 16 * i, *widths(name))
                        if extra:
                            extra(i, j, 2 * u0 + 4 * i)

                    unit(0, 0, split=False)
                    unit(0, 1)
                    with act.Fori(1, dict(SECTIONS)[name] // 2) as i:
                        for j in range(2):
                            unit(i, j)

                def norm(f):
                    begins = ("gu0", "pA", "gu1")[f]
                    split_tile(begins, 0)
                    if f == 0:
                        act.wait_ge(sem["unit_free"], me.at("unit_free", FIRST[begins]))
                        act.sem_inc(sem["held"], 1)
                        act.dma_start(cur[:], t["params"][lay]).then_inc(sem["par_ready"], 16)
                    split_tile(begins, 1)
                    act.wait_ge(sem["ss_ready"], me.at("ss_ready", f + 1))
                    A(tmp[:, 5], bank[4][:], ACT.Ln, bias=eps[:, 0:1]).then_inc(sem["ln_ready"], 1)
                    act.wait_ge(sem["ln_ready"], me.at("ln_ready", f + 1))
                    A(tmp[:, 4], tmp[:, 5], ACT.Exp, scale=-0.5).then_inc(sem["rstd_ready"], 1)
                    for k in range(KD):
                        act.wait_ge(sem["hf_ready"], me.at("hf_ready", f * KD + k + 1))
                        A(hhi[:, k], tmp[:, 2 + k % 2], ACT.Copy).then_inc(sem["hhi_ready"], 1)

                def x_square(name, e, c, t_):
                    per = KD // dict(SECTIONS)[name]
                    act.wait_ge(sem["unit_free"], me.at("unit_free", FIRST[name] + (c + 1 if per == 1 else c)))
                    act.wait_ge(sem["sum_part"], me.at("sum_part", e * KD + (c if per == 1 else 2 * c - 2 + t_) - 1))
                    k = c if per == 1 else 2 * c - 2 + t_
                    A(tmp[:, t_], x[:, k], ACT.Square).then_inc(sem["sq_ready"], 1)

                def down_square(f):
                    def extra(i, j, T):
                        if not (isinstance(i, int) and i == 0 and j == 0):
                            x_square(f"dn{f}", 2 * f, 2 * i + j - 1, 1 - j)
                    return extra

                def out_square(i, j, T):
                    if not (isinstance(i, int) and i == 0 and j == 0):
                        for t_ in range(2):
                            x_square("wo", 1, 2 * i + j, t_)

                def silu(i, j, T):
                    act.wait_ge(sem["tile_done"], me.at("tile_done", T + 1))
                    A(tmp[:, j], bank[2 * j][:], ACT.Silu).then_inc(sem["silu_ready"], 1)

                norm(0)
                section("gu0", silu)
                split_tile("dn0", 0)
                split_tile("dn0", 1)
                section("dn0", down_square(0))
                x_square("dn0", 0, KD - 1, 1)
                norm(1)
                section("pA")
                split_tile("pM0", 0)
                split_tile("pM0", 1)
                def fill(name, plan, n, after=None):
                    for T in ended(plan, n):
                        if T + 2 < len(plan[1]):
                            split_tile(name, T + 2)
                        if after and T % 2 == 0:
                            after(T)

                def gate_unit(b):
                    def after(T):
                        c = T // 2
                        act.wait_ge(sem["tile_done"], me.at("tile_done", 2 * FIRST[f"cb{b}"] + T + 1))
                        if b or c >= 2:
                            act.wait_ge(sem["y_ready"], me.at("y_ready", b * KD + c - 1))
                        A(tmp[:, c % 2], bank[2 * (c % 2)][:], ACT.Sigmoid, bias=par("gbias", c + b * KD)
                          ).then_inc(sem["gate_ready"], 1)
                    return after

                act.wait_ge(sem["zde_ready"], me.next("zde_ready", 2))
                act.wait_ge(sem["con_in"], 48)
                for kv in range(2):
                    for par2 in range(2):
                        for g in range(2):
                            act.dma_start(ee[par2 * HD:(par2 + 1) * HD, kv, g], zde[g * HD:(g + 1) * HD, kv, par2]
                                          ).then_inc(sem["ee_ready"], 16)
                split_tile("pM0", 2)
                act.wait_ge(sem["xf_ready"], me.next("xf_ready", 4))
                A(xhi[:, 0], xf[:].rearrange("p l g c -> p l (g c)"), ACT.Copy).then_inc(sem["xhi_ready"], 1)
                split_tile("pM0", 3)
                act.wait_ge(sem["xf_ready"], me.next("xf_ready", 4))
                A(xhi[:, 1], xf[:].rearrange("p l g c -> p l (g c)"), ACT.Copy).then_inc(sem["xhi_ready"], 1)
                split_tile("cq", 0)
                split_tile("cq", 1)
                act.wait_ge(sem["xlo_ready"], me.next("xlo_ready", 2))

                def square(i, src, n=S):
                    A(tmp[:, 0, 0:n], src, ACT.Square).then_inc(sem["nr_sq"], 1)

                def root(n=S, q=False):
                    act.wait_ge(sem["nr_ss"], me.next("nr_ss"))
                    if me.seen["nr_ss"] > 1:
                        act.wait_ge(sem["nr_rs"], me.at("nr_rs", me.seen["nr_ss"] - 1))
                    A(tmp[:, 1, 0:n], bank[4][:, 0:n], ACT.Ln, scale=float(HD) if q else 1.0, bias=eps[:, int(q):int(q) + 1]
                      ).then_inc(sem["nr_ln"], 1)
                    act.wait_ge(sem["nr_ln"], me.next("nr_ln"))
                    if me.seen["nr_ln"] > 1:
                        act.wait_ge(sem["nr_xn"], me.at("nr_xn", me.seen["nr_ln"] - 1))
                    A(tmp[:, 2, 0:n], tmp[:, 1, 0:n], ACT.Exp, scale=-0.5).then_inc(sem["nr_rs"], 1)

                roped = [KS, KW, Q, Q + 1, Q + 2, Q + 3]
                for i in range(4):
                    if i < 3:
                        square(2 * i, z[:, roped[2 * i]])
                    split_tile("cq", 4 * i + 2)
                    split_tile("cq", 4 * i + 3)
                    if i < 3:
                        root(q=i > 0)
                        square(2 * i + 1, z[:, roped[2 * i + 1]])
                        root(q=i > 0)
                        split_tile("cq", 4 * i + 4)
                        split_tile("cq", 4 * i + 5)
                for i in range(2):
                    act.wait_ge(sem["vt_mm"], me.next("vt_mm"))
                    A(vsw[i], bank[6 + i][:].rearrange("p (a b) -> p a b", a=NB), ACT.Copy).then_inc(sem["vt_ready"], 1)
                act.wait_ge(sem["gx_ready"], me.next("gx_ready"))
                A(gl[:, 0:2], gx[:, 0:2], ACT.Gelu_apprx_tanh).then_inc(sem["gl_ready"], 1)
                act.wait_ge(sem["glr_zero"], me.next("glr_zero"))
                for ht in range(2):
                    A(glr[:, ht, :, :, 0:NCMP], gx[:, 2 + ht].rearrange("p (g c) -> p g c", g=2).unsqueeze(2)
                      .broadcast_to([P, 2, 4, NCMP]), ACT.Gelu_apprx_tanh).then_inc(sem["glr_ready"], 1)
                act.wait_ge(sem["gt_mm"], me.next("gt_mm"))
                A(gt, bank[6][:, 0:NB * 32].rearrange("p (a b) -> p a b", a=NB), ACT.Sigmoid).then_inc(sem["gt_ready"], 1)
                split_tile("pM1", 0)
                act.wait_ge(sem["kc_ready"], me.next("kc_ready"))
                square(6, kcr[:, 0:NCMP], NCMP)
                root(NCMP)
                split_tile("pM1", 1)
                fill("pM1", PM1, 0)
                fill("pM1", PM1, 1)
                for g in range(2):
                    act.wait_ge(sem["cs_sub"], me.next("cs_sub"))
                    A(pc[:, g, :, 0:NCMP], pc[:, g, :, 0:NCMP], ACT.Exp).then_inc(sem["cs_exp"], 1)
                fill("pM1", PM1, 2)
                fill("pM1", PM1, 3)

                def exps(n):
                    w_ = (n % NB + 1) * P
                    for w in range(2):
                        act.wait_ge(sem["s_max"], me.next("s_max"))
                        A(pr[:, n % 2, w, 0:w_], bank[4 + w][:, 0:w_], ACT.Exp, bias=st2[:, n % 2, 0, w:w + 1],
                          accum_out=st2[:, n % 2, 1, w:w + 1]).then_inc(sem["s_exp"], 1)

                exps(0)
                for g in range(2):
                    act.wait_ge(sem["cs_t"], me.next("cs_t"))
                    A(pct[:, g], bank[6 + g][:], ACT.Copy).then_inc(sem["cs_pt"], 1)
                for n in range(8 * NB):
                    w_ = (n % NB + 1) * P
                    for w in range(2):
                        act.wait_ge(sem["s_t"], me.next("s_t"))
                        A(prt[:, n % 2, w, 0:w_], bank[6][:, 0:w_], ACT.Copy).then_inc(sem["s_pt"], 1)
                        if w == 0 and n + 1 < 8 * NB:
                            exps(n + 1)
                        fill("pM1", PM1, 4 + 2 * n + w)
                fill("pM1", PM1, 68)
                split_tile("cb0", 0)
                split_tile("cb0", 1)
                act.wait_ge(sem["row_abs"], me.next("row_abs"))
                A(tmp[0:NH, 3], tmp[0:NH, 2], ACT.Exp, scale=-1.0).then_inc(sem["row_e"], 1)
                act.wait_ge(sem["row_e"], me.at("row_e", 1))
                A(tmp[0:NH, 2], tmp[0:NH, 3], ACT.Ln, bias=ones[0:NH, 0:1]).then_inc(sem["row_l"], 1)
                for n in range(8):
                    fill("cb0", CB, n, gate_unit(0))
                    if n < 4:
                        act.wait_ge(sem["vm_mm"], me.next("vm_mm"))
                        A(zm[:, 4 + n], bank[6 + n % 2][:], ACT.Copy).then_inc(sem["vm_ready"], 1)
                    else:
                        act.wait_ge(sem["cv"], me.next("cv", 4))
                        A(zm[:, n - 4], tmp[:, 3 + n % 2], ACT.Silu).then_inc(sem["cv_silu"], 1)
                for h in range(NH):
                    A(zm[:, 8 + h], zm[:, 8 + h], ACT.Sigmoid).then_inc(sem["og_ready"], 1)
                act.wait_ge(sem["rt_ready"], me.next("rt_ready"))
                for h in range(NH):
                    fill("cb0", CB, 8 + 4 * h, gate_unit(0))
                    if h:
                        act.wait_ge(sem["num_mm"], me.at("num_mm", h))
                        act.wait_ge(sem["den_mm"], me.at("den_mm", h))
                    act.wait_ge(sem["mb_mm"], me.next("mb_mm"))
                    for jt in range(NB - 1):
                        A(dm[jt][:, P:], bank[4][:, (jt + 1) * P:S], ACT.Exp, scale=-1.0, bias=rt[:, jt, h:h + 1])
                    act.wait_ge(sem["md_mm"], me.next("md_mm"))
                    for jt in range(NB):
                        i = A(dm[jt][:, 0:P], bank[5][:, jt * P:(jt + 1) * P], ACT.Exp, scale=-1.0,
                              bias=rt[:, jt, h:h + 1])
                    i.then_inc(sem["d_exp"], 1)
                    act.wait_ge(sem["mm_mm"], me.next("mm_mm"))
                    if h:
                        act.wait_ge(sem["h_out"], me.at("h_out", h))
                    A(tmp[:, 5], bank[6][:], ACT.Exp, scale=-1.0).then_inc(sem["em_exp"], 1)
                    for n in range(1, 4):
                        fill("cb0", CB, 8 + 4 * h + n, gate_unit(0))
                fill("cb0", CB, 24, gate_unit(0))
                split_tile("cb1", 0)
                split_tile("cb1", 1)

                def out_high(b, first, tiles=range(4)):
                    for o in tiles:
                        act.wait_ge(sem["h_gated" if b == 1 else "og_out"], me.at("h_gated" if b == 1 else "og_out", o + 1))
                        if o == 0:
                            act.wait_ge(sem["tile_done"], me.at("tile_done", 2 * FIRST[f"cb{b}"]))
                        A(ohi[:, o], zm[:, first + o], ACT.Copy).then_inc(sem["o_hi"], 1)

                out_high(1, 8)
                for p in range(2):
                    act.wait_ge(sem["al_abs"], me.next("al_abs"))
                    A(tmp[:, 4], tmp[:, 3], ACT.Exp, scale=-1.0).then_inc(sem["al_e"], 1)
                    act.wait_ge(sem["al_e"], me.at("al_e", p + 1))
                    A(tmp[:, 3], tmp[:, 4], ACT.Ln, bias=ones[:, 0:1]).then_inc(sem["al_l"], 1)
                for h in range(NH):
                    fill("cb1", CB, h, gate_unit(1))
                    act.wait_ge(sem["vg_mm"], me.next("vg_mm"))
                    A(zm[:, 16 + h], bank[6 + h % 2][:], ACT.Copy).then_inc(sem["vg_ready"], 1)
                for h in range(NH):
                    A(zm[:, 20 + h], zm[:, 20 + h], ACT.Silu).then_inc(sem["sr_ready"], 1)

                def decays(p, v):
                    act.wait_ge(sem["lv_d"], me.next("lv_d"))
                    if p or v >= 2:
                        act.wait_ge(sem["lv_m"], me.at("lv_m", 9 * p + v - 1 if v >= 2 else 9))
                    A(ge[:, v % 2], tmp[:, 4 + v % 2], ACT.Exp, scale=1.0 / 16).then_inc(sem["lv_e"], 1)

                for p in range(2):
                    decays(p, 0)
                    for v in range(len(LEVELS) + 1):
                        s = LEVELS[v] if v < len(LEVELS) else 0
                        if v + 1 < len(LEVELS):
                            decays(p, v + 1)
                        if s:
                            fill("cb1", CB, 4 + 11 * p + v, gate_unit(1))
                        if s >= P:
                            act.wait_ge(sem["lv_mm"], me.at("lv_mm", 10 * p + v + 1))
                            if p and s == 2 * P:
                                act.wait_ge(sem["og_mm"], me.at("og_mm", 2))
                            for hh in range(2):
                                b = bank[4 + 2 * (v % 2) + hh]
                                if s == 2 * P:
                                    A(ao[:, hh, 0, P:3 * P], b[:, 0:2 * P], ACT.Copy)
                                    i = A(ao[:, hh, 1, 0:2 * P], b[:, 2 * P:4 * P], ACT.Copy)
                                else:
                                    A(ao[:, hh, 0, 0:P], b[:, 0:P], ACT.Copy)
                                    i = A(ao[:, hh, 2, 0:P], b[:, P:2 * P], ACT.Copy)
                                i.then_inc(sem["lv_rect"], 1)
                    if p:
                        fill("cb1", CB, 24, gate_unit(1))
                        split_tile("cb2", 0)
                        split_tile("cb2", 1)
                        out_high(2, 20, (0, 1))
                    for hh in range(2):
                        if p == 0:
                            fill("cb1", CB, 13 + hh, gate_unit(1))
                        act.wait_ge(sem["og_mm"], me.next("og_mm"))
                        A(tmp[:, 2], bank[4 + hh][:], ACT.Square).then_inc(sem["og_sq"], 1)
                        act.wait_ge(sem["og_ss"], me.next("og_ss"))
                        if p or hh:
                            act.wait_ge(sem["og_rs"], me.at("og_rs", 2 * p + hh))
                        A(tmp[:, 3], bank[6][:], ACT.Ln, scale=float(KD), bias=eps[:, 0:1]).then_inc(sem["og_ln"], 1)
                        act.wait_ge(sem["og_ln"], me.next("og_ln"))
                        if hh:
                            act.wait_ge(sem["og_t"], me.at("og_t", 2 * p + hh))
                        A(tmp[:, 4], tmp[:, 3], ACT.Exp, scale=-0.5).then_inc(sem["og_rs"], 1)
                out_high(2, 20, (2, 3))

                def turn(i, j, last=False):
                    u, c = FIRST["cb2"] + j + 2 * i, 2 * i + j
                    act.wait_ge(raw_ready[1 - j], me.at("raw_ready", 8 * (FIRST["cb2"] + 2 * j + 2 * i) + 16))
                    act.wait_ge(sem["tile_done"], me.at("tile_done", 2 * u + 1))
                    A(whi[:, 0, 0:KD * P], raw[:, 1 - j, 0:KD * P], ACT.Copy).then_inc(sem["hi_done"], 1)
                    act.wait_ge(sem["y_ready"], me.at("y_ready", 2 * KD + c - 1))
                    A(tmp[:, j], bank[2 * j][:], ACT.Sigmoid, bias=par("gbias", c + 2 * KD)).then_inc(sem["gate_ready"], 1)
                    act.wait_ge(sem["tile_done"], me.at("tile_done", 2 * u + 2))
                    w = KD * P if last else 4 * P
                    A(whi[:, 1, 0:w], raw[:, 1 - j, KD * P:KD * P + w], ACT.Copy).then_inc(sem["hi_done"], 1)

                with act.Fori(0, KD // 2 - 1) as i:
                    for j in range(2):
                        turn(i, j)
                turn(KD // 2 - 1, 0)
                turn(KD // 2 - 1, 1, last=True)
                act.wait_ge(sem["y_ready"], me.at("y_ready", 3 * KD))
                for k in range(KD):
                    A(yhi[:, k], y[:, k], ACT.Copy).then_inc(sem["yhi_ready"], 1)
                section("wo", out_square)
                for t_ in range(2):
                    x_square("wo", 1, KD // 2, t_)
                norm(2)
                section("gu1", silu)
                split_tile("dn1", 0)
                split_tile("dn1", 1)
                section("dn1", down_square(1))
                x_square("dn1", 2, KD - 1, 1)

        @block.vector
        def _(dve):
            dve.sem_inc(sem["unit_free"], credit["unit_free"])
            dve.wait_ge(sem["con_in"], 48)
            dve.wait_ge(sem["const_set"], 4)
            dve.tensor_copy(masks[:], tmp[:, 2:4].rearrange("p a (b c) -> p (a b) c", c=P)).then_inc(sem["masks_set"], 1)
            dve.wait_ge(sem["masks_set"], 1)
            dve.sem_inc(sem["held"], 1)
            for c in range(KD):
                dve.wait_ge(sem["sq_ready"], c + 1)
                if c:
                    dve.wait_ge(sem["sum_part"], c)
                    dve.tensor_tensor(tmp[:, 4], tmp[:, 4], tmp[:, c % 2], ALU.add).then_inc(sem["sum_part"], 1)
                else:
                    dve.tensor_copy(tmp[:, 4], tmp[:, 0]).then_inc(sem["sum_part"], 1)
            with dve.Fori(0, L) as lay:
                me = Counts(lay)

                def clear_sum():
                    dve.memset(tmp[:, 4], 0.0).then_inc(sem["dve_step"], 1)
                    dve.wait_ge(sem["dve_step"], me.next("dve_step"))
                    dve.sem_inc(sem["held"], 1)

                def add_square(e, c, j):
                    dve.wait_ge(sem["sq_ready"], me.at("sq_ready", e * KD + c + 1))
                    dve.wait_ge(sem["sum_part"], me.at("sum_part", e * KD + c))
                    dve.tensor_tensor(tmp[:, 4], tmp[:, 4], tmp[:, j], ALU.add).then_inc(sem["sum_part"], 1)

                def norm(f):
                    if f == 0:
                        dve.wait_ge(sem["par_ready"], me.at("par_ready", 16))
                    dve.wait_ge(sem["rstd_ready"], me.at("rstd_ready", f + 1))
                    def normed(k):
                        dve.scalar_tensor_tensor(tmp[:, 2 + k % 2], x[:, k], par("norm", f * KD + k), tmp[:, 4],
                                                 ALU.mult, ALU.mult).then_inc(sem["hf_ready"], 1)

                    normed(0)
                    for k in range(KD):
                        if k + 1 < KD:
                            if k:
                                dve.wait_ge(sem["hlo_ready"], me.at("hlo_ready", f * KD + k))
                            normed(k + 1)
                        dve.wait_ge(sem["hhi_ready"], me.at("hhi_ready", f * KD + k + 1))
                        dve.wait_ge(sem["hf_ready"], me.at("hf_ready", f * KD + k + 1))
                        dve.tensor_tensor(hlo[:, k], tmp[:, 2 + k % 2], hhi[:, k].bitcast(f32), ALU.subtract
                                          ).then_inc(sem["hlo_ready"], 1)
                    dve.wait_ge(sem["hlo_ready"], me.at("hlo_ready", (f + 1) * KD))
                    dve.sem_inc(sem["held"], 1)

                def ffn(f):
                    with dve.Fori(0, KF // 2) as i:
                        for j in range(2):
                            n, m, c = FIRST[f"gu{f}"] + j + 2 * i, f * KF + j + 2 * i, 2 * i + j
                            dve.wait_ge(sem["silu_ready"], me.at("silu_ready", m + 1))
                            dve.wait_ge(sem["tile_done"], me.at("tile_done", 2 * n + 2))
                            dve.tensor_tensor(tmp[:, 2 + j], tmp[:, j], bank[2 * j + 1][:], ALU.mult
                                              ).then_inc(sem["unit_free"], 1)
                            dve.wait_ge(sem["unit_free"], me.at("unit_free", n + 1))
                            dve.tensor_copy(uhi[:, c], tmp[:, 2 + j]).then_inc(sem["uhi_ready"], 1)
                            dve.wait_ge(sem["uhi_ready"], me.at("uhi_ready", m + 1))
                            dve.tensor_tensor(ulo[:, c], tmp[:, 2 + j], uhi[:, c].bitcast(f32), ALU.subtract
                                              ).then_inc(sem["ulo_ready"], 1)
                    clear_sum()
                    with dve.Fori(0, KD // 2) as i:
                        for j in range(2):
                            n, c = FIRST[f"dn{f}"] + j + 2 * i, 2 * i + j
                            dve.wait_ge(sem["tile_done"], me.at("tile_done", 2 * n + 2))
                            dve.scalar_tensor_tensor(x[:, c], bank[2 * j][:], 0.5, x[:, c], ALU.mult, ALU.add
                                                     ).then_inc(sem["unit_free"], 1)
                            add_square(2 * f, c, j)
                    dve.wait_ge(sem["unit_free"], me.at("unit_free", FIRST[f"dn{f}"] + KD))
                    dve.sem_inc(sem["held"], 1)

                def project(name, dst, first, bias):
                    with dve.Fori(0, dict(SECTIONS)[name] // 2) as i:
                        for j in range(2):
                            u, c = FIRST[name] + j + 2 * i, first + 4 * i + 2 * j
                            dve.wait_ge(sem["tile_done"], me.at("tile_done", 2 * u + 1))
                            dve.tensor_scalar(dst[:, c], bank[2 * j][:], par("bias", bias + c), None, ALU.add)
                            dve.wait_ge(sem["tile_done"], me.at("tile_done", 2 * u + 2))
                            dve.tensor_scalar(dst[:, c + 1], bank[2 * j + 1][:], par("bias", bias + c + 1),
                                              None, ALU.add).then_inc(sem["unit_free"], 1)
                    dve.wait_ge(sem["unit_free"], me.at("unit_free", FIRST[name] + dict(SECTIONS)[name]))
                    dve.sem_inc(sem["held"], 1)

                def group_tile(u, s, c):
                    dve.wait_ge(sem["tile_done"], me.at("tile_done", 2 * u + s + 1))
                    i = dve.tensor_scalar(zm[:, c], bank[2 * (u % 2) + s][:], par("bias", GT_TILES + c), None, ALU.add)
                    if s:
                        i.then_inc(sem["unit_free"], 1)

                def fill_group(n):
                    for T in ended(PM1, n):
                        group_tile(FIRST["pM1"] + T // 2, T % 2, MT_TILES - 12 + T)

                def combine_unit(b, j, u, c):
                    dve.wait_ge(sem["gate_ready"], me.at("gate_ready", b * KD + c + 1))
                    dve.wait_ge(sem["tile_done"], me.at("tile_done", 2 * u + 2))
                    dve.tensor_tensor(tmp[:, j] if b else y[:, c], tmp[:, j], bank[2 * j + 1][:], ALU.mult
                                      ).then_inc(sem["unit_free"], 1)
                    dve.wait_ge(sem["unit_free"], me.at("unit_free", u + 1))
                    if b:
                        dve.tensor_tensor(y[:, c], y[:, c], tmp[:, j], ALU.add).then_inc(sem["y_ready"], 1)
                    else:
                        dve.sem_inc(sem["y_ready"], 1)

                def fill_combine(b, n):
                    for T in ended(CB, n):
                        if T % 2:
                            combine_unit(b, T // 2 % 2, FIRST[f"cb{b}"] + T // 2, T // 2)

                norm(0)
                ffn(0)
                norm(1)
                project("pA", z, 0, 0)
                for kv in range(2):
                    dve.tensor_copy(zde[:, kv], z[:, KC + kv].rearrange("p (m a) -> p a m", a=2)).then_inc(sem["zde_ready"], 1)
                dve.memset(glr[:], 0.0).then_inc(sem["glr_zero"], 1)
                dve.wait_ge(sem["ee_ready"], me.at("ee_ready", 128))

                def blocks(kv):
                    for g in range(2):
                        for half in range(2):
                            src = ee[:, kv, g].rearrange("p (c l) -> p l c", l=8)[:, :, half:half + NCMP]
                            pe_ = par("pe", 16 * kv + 8 * half, 8).unsqueeze(2).broadcast_to([P, 8, NCMP])
                            dve.tensor_tensor(xf[:, 8 * half:8 * half + 8, g], src, pe_, ALU.add).then_inc(sem["xf_ready"], 1)

                def blocks_low(kv):
                    dve.wait_ge(sem["xhi_ready"], me.next("xhi_ready"))
                    dve.wait_ge(sem["xf_ready"], me.at("xf_ready", 4 * kv + 4))
                    dve.tensor_tensor(xlo[:, kv], xf[:].rearrange("p l g c -> p l (g c)"), xhi[:, kv].bitcast(f32),
                                      ALU.subtract).then_inc(sem["xlo_ready"], 1)
                    dve.wait_ge(sem["xlo_ready"], me.next("xlo_ready"))

                blocks(0)
                blocks_low(0)
                blocks(1)
                group_tile(FIRST["pM0"], 0, 0)
                group_tile(FIRST["pM0"], 1, 1)
                blocks_low(1)
                group_tile(FIRST["pM0"] + 1, 0, 2)
                group_tile(FIRST["pM0"] + 1, 1, 3)

                def normed_tile(src, n, gain, co):
                    dve.wait_ge(sem["nr_rs"], me.next("nr_rs"))
                    dve.scalar_tensor_tensor(tmp[:, 3, 0:n], src, par("qkn", gain), tmp[:, 2, 0:n],
                                             ALU.mult, ALU.mult).then_inc(sem["nr_xn"], 1)
                    dve.wait_ge(sem["nr_xn"], me.next("nr_xn"))
                    dve.tensor_tensor(tmp[:, 5, 0:n], tmp[:, 3, 0:n], co, ALU.mult).then_inc(sem["nr_parts"], 1)

                def roped_tile(dst, n, si):
                    dve.wait_ge(sem["nr_rot"], me.next("nr_rot"))
                    dve.tensor_tensor(tmp[:, 4, 0:n], bank[5][:, 0:n], si, ALU.mult).then_inc(sem["nr_parts"], 1)
                    dve.wait_ge(sem["nr_parts"], me.next("nr_parts", 2))
                    dve.tensor_tensor(dst, tmp[:, 4, 0:n], tmp[:, 5, 0:n], ALU.add).then_inc(sem["nr_out"], 1)
                    dve.wait_ge(sem["nr_out"], me.next("nr_out"))

                roped = [(KS, 2), (KW, 3)] + [(Q + i, 0) for i in range(4)]
                for i in range(4):
                    u = FIRST["cq"] + 2 * i
                    if i < 3:
                        normed_tile(z[:, roped[2 * i][0]], S, roped[2 * i][1], cos)
                    dve.wait_ge(sem["tile_done"], me.at("tile_done", 2 * u + 2))
                    dve.tensor_copy(gx[:, i], bank[0][:, 0:2 * NCMP]).then_inc(sem["unit_free"], 1)
                    if i < 3:
                        roped_tile(z[:, roped[2 * i][0]], S, sin)
                        normed_tile(z[:, roped[2 * i + 1][0]], S, roped[2 * i + 1][1], cos)
                        group_tile(u + 1, 0, 4 + 2 * i)
                        roped_tile(z[:, roped[2 * i + 1][0]], S, sin)
                        group_tile(u + 1, 1, 5 + 2 * i)
                dve.wait_ge(sem["unit_free"], me.at("unit_free", FIRST["cq"] + 7))
                dve.sem_inc(sem["gx_ready"], 1)
                group_tile(FIRST["cq"] + 7, 0, 10)
                dve.wait_ge(sem["xlo_ready"], me.at("xlo_ready", 2))
                dve.memset(pc[:], 0.0).then_inc(sem["dve_step"], 1)
                dve.wait_ge(sem["dve_step"], me.next("dve_step"))
                dve.wait_ge(sem["kc_mm"], me.next("kc_mm"))
                dve.tensor_copy(kcr[:, 0:NCMP], bank[5][:, 0:NCMP]).then_inc(sem["kc_ready"], 1)
                dve.wait_ge(sem["kc_ready"], me.next("kc_ready"))
                dve.wait_ge(sem["vc_mm"], me.next("vc_mm"))
                dve.tensor_copy(vcr, bank[7][:, 0:P]).then_inc(sem["vc_ready"], 1)
                group_tile(FIRST["cq"] + 7, 1, 11)
                normed_tile(kcr[:, 0:NCMP], NCMP, 1, cc("ccos", NCMP))
                roped_tile(kcr[:, 0:NCMP], NCMP, cc("csin", NCMP))
                fill_group(0)
                fill_group(1)
                fill_group(2)
                dve.wait_ge(sem["gt_ready"], me.at("gt_ready", 1))
                for g in range(2):
                    dve.wait_ge(sem["cs_mm"], me.next("cs_mm"))
                    cs = bank[6 + g][:].rearrange("p (a c) -> p a c", c=32)[:, :, 0:NCMP]
                    pg = pc[:, g, :, 0:NCMP]
                    wide = lambda v: v.unsqueeze(2).broadcast_to([P, NB * 4, NCMP])
                    dve.tensor_reduce(st4[:, 0], cs, AX.X, ALU.max).then_inc(sem["dve_step"], 1)
                    dve.wait_ge(sem["dve_step"], me.next("dve_step"))
                    dve.tensor_scalar(st4[:, 1], st4[:, 0], -1e20, None, ALU.max).then_inc(sem["dve_step"], 1)
                    dve.wait_ge(sem["dve_step"], me.next("dve_step"))
                    dve.tensor_tensor(pg, cs, wide(st4[:, 1]), ALU.subtract).then_inc(sem["cs_sub"], 1)
                    dve.wait_ge(sem["cs_sub"], me.next("cs_sub"))
                for g in range(2):
                    pg = pc[:, g, :, 0:NCMP]
                    dve.wait_ge(sem["cs_exp"], me.next("cs_exp"))
                    dve.tensor_reduce(st4[:, 2], pg, AX.X, ALU.add).then_inc(sem["dve_step"], 1)
                    dve.wait_ge(sem["dve_step"], me.next("dve_step"))
                    dve.tensor_scalar(st4[:, 2], st4[:, 2], 1e-30, None, ALU.max).then_inc(sem["dve_step"], 1)
                    dve.wait_ge(sem["dve_step"], me.next("dve_step"))
                    dve.reciprocal(st4[:, 3], st4[:, 2]).then_inc(sem["dve_step"], 1)
                    dve.wait_ge(sem["dve_step"], me.next("dve_step"))
                    dve.tensor_tensor(st4[:, 3].rearrange("p (i t) -> p i t", t=4), st4[:, 3].rearrange("p (i t) -> p i t", t=4),
                                      gt[:, :, 12 * g:12 * g + 12].rearrange("p i (t k) -> p i t k", k=3)[:, :, :, 0],
                                      ALU.mult).then_inc(sem["dve_step"], 1)
                    dve.wait_ge(sem["dve_step"], me.next("dve_step"))
                    dve.tensor_tensor(pg, pg, wide(st4[:, 3]), ALU.mult).then_inc(sem["cs_out"], 1)
                    dve.wait_ge(sem["cs_out"], me.next("cs_out"))
                fill_group(3)

                def maxima(n):
                    for w in range(2):
                        dve.wait_ge(sem["s_mm"], me.next("s_mm"))
                        dve.tensor_reduce(st2[:, n % 2, 0, w:w + 1], bank[4 + w][:, 0:(n % NB + 1) * P], AX.X, ALU.max,
                                          negate=True).then_inc(sem["s_max"], 1)

                def nsa_parts(tt):
                    dve.wait_ge(sem["pv"], me.at("pv", 8 * tt + 8))
                    dve.tensor_copy(ohi[:, tt], bank[7][:]).then_inc(sem["o_hi"], 1)
                    dve.wait_ge(sem["o_hi"], me.next("o_hi"))
                    dve.tensor_tensor(olo[:, tt], bank[7][:], ohi[:, tt].bitcast(f32), ALU.subtract).then_inc(sem["o_lo"], 1)

                maxima(0)
                for n in range(8 * NB):
                    b, it = n // NB, n % NB
                    head = b // 2 + 4 * (b % 2)
                    dve.wait_ge(sem["s_exp"], me.next("s_exp", 2))
                    dve.reciprocal(st2[:, n % 2, 2], st2[:, n % 2, 1]).then_inc(sem["dve_step"], 1)
                    dve.wait_ge(sem["dve_step"], me.next("dve_step"))
                    dve.tensor_tensor(st2[:, n % 2, 3], st2[:, n % 2, 2],
                                      gt[:, it, 3 * head + 1:3 * head + 3], ALU.mult).then_inc(sem["dve_step"], 1)
                    dve.wait_ge(sem["dve_step"], me.next("dve_step"))
                    for w in range(2):
                        dve.tensor_scalar(pr[:, n % 2, w, 0:(it + 1) * P], pr[:, n % 2, w, 0:(it + 1) * P],
                                          st2[:, n % 2, 3, w:w + 1], None, ALU.mult).then_inc(sem["s_p"], 1)
                    if n and n % 8 == 0:
                        nsa_parts(n // 8 - 1)
                    if n + 1 < 8 * NB:
                        maxima(n + 1)
                    fill_group(4 + 2 * n)
                    fill_group(5 + 2 * n)
                fill_group(68)
                nsa_parts(3)
                dve.scalar_tensor_tensor(tmp[0:NH, 2], small[R_F:R_F + NH], -1.0, small[R_F:R_F + NH], ALU.mult, ALU.max).then_inc(sem["row_abs"], 1)
                dve.tensor_copy(tmp[0:NH, 4], small[R_I:R_I + NH]).then_inc(sem["dve_step"], 1)
                dve.wait_ge(sem["dve_step"], me.next("dve_step"))
                dve.wait_ge(sem["row_l"], me.next("row_l"))
                dve.scalar_tensor_tensor(tmp[0:NH, 3], small[R_F:R_F + NH], 0.0, tmp[0:NH, 2], ALU.min, ALU.subtract).then_inc(sem["dve_step"], 1)
                dve.wait_ge(sem["dve_step"], me.next("dve_step"))
                one = ones[0:NH, 0:1].broadcast_to([NH, S])
                dve.tensor_tensor_scan(tmp[0:NH, 5], one, tmp[0:NH, 3], 0.0, ALU.mult, ALU.add).then_inc(sem["dve_step"], 1)
                dve.wait_ge(sem["dve_step"], me.next("dve_step"))
                dve.tensor_tensor(row0[:], tmp[0:NH, 4], tmp[0:NH, 5], ALU.subtract).then_inc(sem["dve_step"], 1)
                dve.wait_ge(sem["dve_step"], me.next("dve_step"))
                dve.tensor_tensor_scan(rows[:, 0], one, row0[:], 0.0, ALU.mult, ALU.max).then_inc(sem["dve_step"], 1)
                dve.wait_ge(sem["dve_step"], me.next("dve_step"))
                dve.tensor_tensor(rows[:, 1], tmp[0:NH, 5], rows[:, 0], ALU.add).then_inc(sem["row_m"], 1)
                dve.wait_ge(sem["row_m"], me.next("row_m"))
                for n in range(4):
                    fill_combine(0, n)
                for c in range(4):
                    acc = tmp[:, 3 + c % 2]
                    if c >= 2:
                        dve.wait_ge(sem["cv_silu"], me.at("cv_silu", c - 1))
                    dve.tensor_scalar(acc, zm[:, c], par("convw", 4 * c + 3), par("convb", c), ALU.mult, ALU.add).then_inc(sem["cv"], 1)
                    dve.wait_ge(sem["cv"], me.next("cv"))
                    for d in (1, 2, 3):
                        dve.scalar_tensor_tensor(acc[:, d:S], zm[:, c, 0:S - d], par("convw", 4 * c + 3 - d),
                                                 acc[:, d:S], ALU.mult, ALU.add).then_inc(sem["cv"], 1)
                        dve.wait_ge(sem["cv"], me.next("cv"))
                    fill_combine(0, 4 + c)
                dve.wait_ge(sem["rt_mm"], me.next("rt_mm"))
                dve.tensor_copy(rt[:].rearrange("p a b -> p (a b)"), bank[4][:, 0:NB * NH]).then_inc(sem["rt_ready"], 1)
                for h in range(NH):
                    fill_combine(0, 8 + 4 * h)
                    dve.wait_ge(sem["d_exp"], me.next("d_exp"))
                    for jt in range(NB):
                        if jt < 3:
                            dve.wait_ge(sem["sm_mm"], me.next("sm_mm"))
                        src = (bank[7][:, 0:S], bank[6][:, 0:3 * P], bank[4][:, 0:2 * P], bank[4][:, 2 * P:3 * P])[jt]
                        dve.scalar_tensor_tensor(dm[jt], src, HD ** -0.5, dm[jt],
                                                 ALU.mult, ALU.mult).then_inc(sem["sd_mul"], 1)
                    fill_combine(0, 9 + 4 * h)
                    fill_combine(0, 10 + 4 * h)
                    dve.wait_ge(sem["den_mm"], me.next("den_mm"))
                    dve.wait_ge(sem["em_exp"], me.next("em_exp"))
                    dve.scalar_tensor_tensor(tmp[:, 5], bank[6][:], -1.0, tmp[:, 5], ALU.mult, ALU.max).then_inc(sem["dve_step"], 1)
                    dve.wait_ge(sem["dve_step"], me.next("dve_step"))
                    dve.tensor_tensor(tmp[:, 5], bank[6][:], tmp[:, 5], ALU.max).then_inc(sem["dve_step"], 1)
                    dve.wait_ge(sem["dve_step"], me.next("dve_step"))
                    dve.reciprocal(tmp[:, 4], tmp[:, 5]).then_inc(sem["dve_step"], 1)
                    dve.wait_ge(sem["dve_step"], me.next("dve_step"))
                    dve.wait_ge(sem["num_mm"], me.next("num_mm"))
                    dve.tensor_tensor(tmp[:, 3], bank[5][:], tmp[:, 4], ALU.mult).then_inc(sem["h_out"], 1)
                    dve.wait_ge(sem["h_out"], me.next("h_out"))
                    dve.wait_ge(sem["og_ready"], me.at("og_ready", h + 1))
                    dve.tensor_tensor(zm[:, 8 + h], tmp[:, 3], zm[:, 8 + h], ALU.mult).then_inc(sem["h_gated"], 1)
                    dve.wait_ge(sem["h_gated"], me.next("h_gated"))
                    fill_combine(0, 11 + 4 * h)
                fill_combine(0, 24)

                def out_low(b, first, tiles=range(4)):
                    for o in tiles:
                        dve.wait_ge(sem["o_hi"], me.next("o_hi"))
                        dve.tensor_tensor(olo[:, o], zm[:, first + o], ohi[:, o].bitcast(f32), ALU.subtract
                                          ).then_inc(sem["o_lo"], 1)
                    dve.wait_ge(sem["o_lo"], me.at("o_lo", 4 * b + tiles[-1] + 1))

                out_low(1, 8)
                for p in range(2):
                    dve.wait_ge(sem["al_mm"], me.next("al_mm"))
                    dve.tensor_scalar(tmp[:, 2], bank[4 + p][:], par("balpha", p), None, ALU.add).then_inc(sem["dve_step"], 1)
                    dve.wait_ge(sem["dve_step"], me.next("dve_step"))
                    dve.scalar_tensor_tensor(tmp[:, 3], tmp[:, 2], -1.0, tmp[:, 2], ALU.mult, ALU.max).then_inc(sem["al_abs"], 1)
                    dve.wait_ge(sem["al_abs"], me.next("al_abs"))
                    dve.wait_ge(sem["al_l"], me.next("al_l"))
                    dve.scalar_tensor_tensor(tmp[:, 4], tmp[:, 2], 0.0, tmp[:, 3], ALU.min, ALU.subtract).then_inc(sem["dve_step"], 1)
                    dve.wait_ge(sem["dve_step"], me.next("dve_step"))
                    dve.tensor_tensor_scan(bcum[:, p], ones[:, 0:1].broadcast_to([P, S]), tmp[:, 4], 0.0,
                                           ALU.mult, ALU.add).then_inc(sem["al_b"], 1)
                    dve.wait_ge(sem["al_b"], me.next("al_b"))
                    dve.tensor_scalar(zm[:, 12 + p], zm[:, 12 + p], HD ** -0.5, None, ALU.mult).then_inc(sem["dve_step"], 1)
                    dve.wait_ge(sem["dve_step"], me.next("dve_step"))
                dve.memset(ad[:], 0.0).then_inc(sem["ad_zero"], 1)
                dve.wait_ge(sem["ad_zero"], me.next("ad_zero"))
                for n in range(4):
                    fill_combine(1, n)
                for p in range(2):
                    def emit(v):
                        dve.wait_ge(sem["lv_mm"], me.at("lv_mm", 10 * p + v + 1))
                        if p and v == 2:
                            dve.wait_ge(sem["og_mm"], me.at("og_mm", 2))
                        for hh in range(2):
                            m = masks[:, v - 2].unsqueeze(1).broadcast_to([P, NB, P])
                            data = bank[4 + 2 * (v % 2) + hh][:].rearrange("p (a b) -> p a b", a=NB)
                            dve.sem_inc(sem["held"], 1)
                            dve.copy_predicated(ad[:, hh], m, data).then_inc(sem["lv_out"], 1)
                            dve.wait_ge(sem["lv_out"], me.next("lv_out"))

                    def halves(v, t_):
                        return t_.rearrange("p (n h s) -> p n h s", h=2, s=LEVELS[v])

                    def distances(v):
                        B, D = halves(v, bcum[:, p]), halves(v, tmp[:, 4 + v % 2])
                        mid = B[:, :, 0, LEVELS[v] - 1:LEVELS[v]].broadcast_to([P, S // (2 * LEVELS[v]), LEVELS[v]])
                        if v >= 2:
                            dve.wait_ge(sem["lv_e"], me.at("lv_e", 9 * p + v - 1))
                        dve.tensor_tensor(D[:, :, 0], mid, B[:, :, 0], ALU.subtract).then_inc(sem["dve_step"], 1)
                        dve.wait_ge(sem["dve_step"], me.next("dve_step"))
                        dve.tensor_tensor(D[:, :, 1], B[:, :, 1], mid, ALU.subtract).then_inc(sem["lv_d"], 1)

                    distances(0)
                    for v in range(len(LEVELS)):
                        E, M = halves(v, ge[:, v % 2]), halves(v, tmp[:, 2 + v % 2])
                        q, k = halves(v, zm[:, 12 + p]), halves(v, zm[:, 14 + p])
                        if v + 1 < len(LEVELS):
                            distances(v + 1)
                        dve.wait_ge(sem["lv_e"], me.next("lv_e"))
                        if v >= 2:
                            dve.wait_ge(sem["lv_mm"], me.at("lv_mm", 10 * p + v - 1))
                        elif p and v == 0:
                            dve.wait_ge(sem["og_t"], me.at("og_t", 2))
                        dve.tensor_tensor(M[:, :, 0], E[:, :, 0], k[:, :, 0], ALU.mult).then_inc(sem["dve_step"], 1)
                        dve.wait_ge(sem["dve_step"], me.next("dve_step"))
                        dve.tensor_tensor(M[:, :, 1], E[:, :, 1], q[:, :, 1], ALU.mult).then_inc(sem["lv_m"], 1)
                        dve.wait_ge(sem["lv_m"], me.next("lv_m"))
                        if v >= 3:
                            emit(v - 1)
                        fill_combine(1, 4 + 11 * p + v)
                    emit(8)
                    emit(9)
                    for hh in range(2):
                        h = 2 * p + hh
                        if p == 0:
                            fill_combine(1, 13 + hh)
                        elif hh == 0:
                            fill_combine(1, 24)
                            out_low(2, 20, (0, 1))
                        dve.wait_ge(sem["og_rs"], me.next("og_rs"))
                        dve.scalar_tensor_tensor(tmp[:, 5], bank[4 + hh][:], par("gn"), tmp[:, 4], ALU.mult, ALU.mult).then_inc(sem["og_t"], 1)
                        dve.wait_ge(sem["og_t"], me.next("og_t"))
                        dve.wait_ge(sem["sr_ready"], me.at("sr_ready", h + 1))
                        dve.tensor_tensor(zm[:, 20 + h], tmp[:, 5], zm[:, 20 + h], ALU.mult).then_inc(sem["og_out"], 1)
                        dve.wait_ge(sem["og_out"], me.next("og_out"))
                out_low(2, 20, (2, 3))
                dve.sem_inc(sem["held"], 1)
                with dve.Fori(0, KD // 2) as i:
                    for j in range(2):
                        combine_unit(2, j, FIRST["cb2"] + j + 2 * i, 2 * i + j)
                dve.wait_ge(sem["y_ready"], me.at("y_ready", 3 * KD))
                for k in range(KD):
                    dve.wait_ge(sem["yhi_ready"], me.at("yhi_ready", k + 1))
                    dve.tensor_tensor(ylo[:, k], y[:, k], yhi[:, k].bitcast(f32), ALU.subtract).then_inc(sem["ylo_ready"], 1)
                dve.wait_ge(sem["ylo_ready"], me.at("ylo_ready", KD))
                dve.sem_inc(sem["held"], 1)
                clear_sum()
                with dve.Fori(0, 2) as i:
                    for j in range(2):
                        u, c = FIRST["wo"] + j + 2 * i, 4 * i + 2 * j
                        dve.wait_ge(sem["tile_done"], me.at("tile_done", 2 * u + 1))
                        dve.tensor_tensor(x[:, c], bank[2 * j][:], x[:, c], ALU.add)
                        dve.wait_ge(sem["tile_done"], me.at("tile_done", 2 * u + 2))
                        dve.tensor_tensor(x[:, c + 1], bank[2 * j + 1][:], x[:, c + 1], ALU.add).then_inc(sem["unit_free"], 1)
                        add_square(1, c, 0)
                        add_square(1, c + 1, 1)
                dve.wait_ge(sem["unit_free"], me.at("unit_free", FIRST["gu1"]))
                dve.sem_inc(sem["held"], 1)
                norm(2)
                ffn(1)

        @block.tensor
        def _(pe):
            mm = pe.matmul
            pe.sem_inc(sem["tile_done"], credit["tile_done"])
            pe.wait_ge(sem["const_set"], 4)
            pe.wait_ge(sem["con_in"], 48)
            with pe.Fori(0, L) as lay:
                me = Counts(lay)

                def step(T, s, outp, parts, k, free=None, start=True, stop=True, ready=None):
                    if ready:
                        pe.wait_ge(sem[ready[0]], me.at(ready[0], ready[1] + k + 1))
                    if k == 0:
                        pe.wait_ge(sem["lo_done"], me.at("lo_done", T + s + 1))
                        if free is not None:
                            pe.wait_ge(sem["unit_free"], me.at("unit_free", free))
                    mhi, mlo = parts[k]
                    wh, wl = whi[:, s, k * P:(k + 1) * P], wlo[:, s, k * P:(k + 1) * P]
                    mm(outp, wh, mhi, start=start and k == 0, stop=False)
                    mm(outp, wh, mlo, start=False, stop=False)
                    i = mm(outp, wl, mhi, start=False, stop=stop and k == len(parts) - 1)
                    if k == len(parts) - 1:
                        i.then_inc(sem["tile_done"], 1)

                def tile(T, s, outp, parts, free=None, start=True, stop=True, ready=None):
                    for k in range(len(parts)):
                        step(T, s, outp, parts, k, free, start, stop, ready)

                def section(name, a, b, one=False, ready=None, started=False):
                    def unit(i, j, ready=None, started=False):
                        u = FIRST[name] + j + 2 * i
                        if not started:
                            tile(2 * u, 0, bank[2 * j][:], a, free=u - 1, stop=not one, ready=ready)
                        second = ready if started else (ready[0], ready[1] + len(a)) if ready and one else None
                        tile(2 * u, 1, bank[2 * j + (not one)][:], b, start=not one, ready=second)

                    peel = ready is not None or started
                    if peel:
                        unit(0, 0, ready, started)
                        pe.sem_inc(sem["held"], 1)
                        unit(0, 1)
                    with pe.Fori(int(peel), dict(SECTIONS)[name] // 2) as i:
                        for j in range(2):
                            unit(i, j)

                def fill(name, plan, parts, n):
                    at, ends = plan
                    for c in range(at[n], at[n + 1]):
                        T = min(i for i, e in enumerate(ends) if c < e)
                        u, s = FIRST[name] + T // 2, T % 2
                        step(2 * u, s, bank[2 * (u % 2) + s][:], parts[s], c - (ends[T - 1] if T else 0),
                             free=u - 1 if s == 0 else None)

                hp = [(hhi[:, k], hlo[:, k]) for k in range(KD)]
                up = [(uhi[:, k], ulo[:, k]) for k in range(KF)]
                op = [(ohi[:, k], olo[:, k]) for k in range(4)]
                yp = [(yhi[:, k], ylo[:, k]) for k in range(KD)]

                def norm(f):
                    pe.wait_ge(sem["sum_part"], me.at("sum_part", f * KD))
                    mm(bank[4][:], onesm[:], tmp[:, 4], start=True, stop=True).then_inc(sem["ss_ready"], 1)

                def ffn(f):
                    section(f"gu{f}", hp, hp, ready=("hlo_ready", 2 * f * KD))
                    section(f"dn{f}", up[:KF // 2], up[KF // 2:], one=True, ready=("ulo_ready", f * KF))

                def transposes(dst, src):
                    for a in range(NB):
                        i = pe.transpose(dst[:, a * P:(a + 1) * P], src[:, a * P:(a + 1) * P], ident)
                    return i

                norm(0)
                ffn(0)
                norm(1)
                section("pA", hp, hp, ready=("hlo_ready", KD))
                section("pM0", hp, hp)
                pe.wait_ge(sem["xlo_ready"], me.next("xlo_ready", 2))

                def ss(i, n=S):
                    pe.wait_ge(sem["nr_sq"], me.next("nr_sq"))
                    if i:
                        pe.wait_ge(sem["nr_ln"], me.next("nr_ln"))
                    mm(bank[4][:, 0:n], blk, tmp[:, 0, 0:n], start=True, stop=True).then_inc(sem["nr_ss"], 1)

                def rotated(i, n=S):
                    pe.wait_ge(sem["nr_xn"], me.next("nr_xn"))
                    if i:
                        pe.wait_ge(sem["nr_out"], me.next("nr_out"))
                    mm(bank[5][:, 0:n], rot, tmp[:, 3, 0:n], start=True, stop=True).then_inc(sem["nr_rot"], 1)

                for i in range(4):
                    kv, ht = i // 2, i % 2
                    u = FIRST["cq"] + 2 * i
                    for s in range(2):
                        tile(2 * u, s, bank[0][:, 0:2 * NCMP], [(xhi[:, kv, 8 * s + l], xlo[:, kv, 8 * s + l]) for l in range(8)],
                             free=u - 1 if s == 0 else None, start=s == 0, stop=s == 1)
                    if i < 3:
                        ss(2 * i)
                        tile(2 * u + 2, 0, bank[2][:], hp, free=u)
                        rotated(2 * i)
                        ss(2 * i + 1)
                        tile(2 * u + 2, 1, bank[3][:], hp)
                        rotated(2 * i + 1)
                u = FIRST["cq"] + 7
                transposes(bank[6], z[:, VS]).then_inc(sem["vt_mm"], 1)
                transposes(bank[7], z[:, VW]).then_inc(sem["vt_mm"], 1)
                tile(2 * u, 0, bank[2][:], hp, free=u - 1)
                pe.wait_ge(sem["nr_out"], me.next("nr_out"))
                pe.wait_ge(sem["nr_ln"], me.next("nr_ln"))
                pe.wait_ge(sem["gl_ready"], me.next("gl_ready"))
                for g in range(2):
                    for ht in range(2):
                        i = mm(bank[5][g * HD:(g + 1) * HD, 0:NCMP], par("w2", ht * HD, HD),
                               gl[:, ht, g * NCMP:(g + 1) * NCMP], start=ht == 0, stop=ht == 1)
                i.then_inc(sem["kc_mm"], 1)
                pe.wait_ge(sem["glr_ready"], me.next("glr_ready", 2))
                pe.wait_ge(sem["vt_ready"], me.next("vt_ready", 2))
                for g in range(2):
                    for ht in range(2):
                        i = mm(bank[7][:, g * HD:(g + 1) * HD], glr[:, ht, g].rearrange("p a c -> p (a c)"),
                               par("w2", 128 + ht * HD, HD), start=ht == 0, stop=ht == 1)
                i.then_inc(sem["vc_mm"], 1)
                for a in range(NB):
                    i = pe.transpose(bank[6][:, a * 32:(a + 1) * 32], small[R_G:R_G + 32, a * P:(a + 1) * P],
                                     ident[R_G:R_G + 32, R_G:R_G + 32])
                i.then_inc(sem["gt_mm"], 1)
                tile(2 * u, 1, bank[3][:], hp)
                pe.wait_ge(sem["kc_ready"], me.next("kc_ready"))
                pe.wait_ge(sem["nr_sq"], me.next("nr_sq"))
                mm(bank[4][:, 0:NCMP], blk, tmp[:, 0, 0:NCMP], start=True, stop=True).then_inc(sem["nr_ss"], 1)
                fill("pM1", PM1, (hp, hp), 0)
                pe.wait_ge(sem["nr_xn"], me.next("nr_xn"))
                mm(bank[5][:, 0:NCMP], rot, tmp[:, 3, 0:NCMP], start=True, stop=True).then_inc(sem["nr_rot"], 1)
                fill("pM1", PM1, (hp, hp), 1)
                pe.wait_ge(sem["nr_out"], me.next("nr_out"))
                pe.wait_ge(sem["vc_ready"], me.next("vc_ready"))
                pe.wait_ge(sem["gt_ready"], me.next("gt_ready"))
                for g in range(2):
                    r = slice(g * HD, (g + 1) * HD)
                    for it in range(NB):
                        cs = bank[6 + g][:, it * P:(it + 1) * P].rearrange("p (t c) -> p t c", c=32)[:, :, 0:NCMP]
                        mm(cs, identb, mask_cmp[:, it].unsqueeze(1).broadcast_to([P, 4, NCMP]), start=True, stop=False)
                        for tt in range(4):
                            i = mm(cs[:, tt], z[r, Q + tt, it * P:(it + 1) * P], kcr[r, 0:NCMP], start=False, stop=tt == 3)
                    i.then_inc(sem["cs_mm"], 1)

                def scores(n, w):
                    b, it = n // NB, n % NB
                    r = slice(b % 2 * HD, (b % 2 + 1) * HD)
                    if n:
                        pe.wait_ge(sem["s_exp"], me.at("s_exp", 2 * n - 1 + w))
                    mm(bank[4 + w][:, 0:(it + 1) * P], z[r, Q + b // 2, it * P:(it + 1) * P], z[r, KS + w, 0:(it + 1) * P],
                       start=True, stop=False)
                    mm(bank[4 + w][:, it * P:(it + 1) * P], identb, mask_ij, start=False, stop=True).then_inc(sem["s_mm"], 1)

                fill("pM1", PM1, (hp, hp), 2)
                scores(0, 0)
                scores(0, 1)
                fill("pM1", PM1, (hp, hp), 3)
                for g in range(2):
                    pe.wait_ge(sem["cs_out"], me.next("cs_out"))
                    if g == 0:
                        pe.sem_inc(sem["held"], 1)
                    for it in range(NB):
                        i = pe.transpose(bank[6 + g][:, it * P:(it + 1) * P],
                                         pc[:, g, 4 * it:4 * it + 4].rearrange("p t c -> p (t c)"), ident)
                    i.then_inc(sem["cs_t"], 1)
                pe.wait_ge(sem["cs_pt"], me.next("cs_pt", 2))
                def values(n):
                    b, it = n // NB, n % NB
                    tt, g = b // 2, b % 2
                    r = slice(g * HD, (g + 1) * HD)
                    if g == 0 and it == 0 and tt:
                        pe.wait_ge(sem["o_lo"], me.at("o_lo", tt))
                    pe.wait_ge(sem["s_pt"], me.at("s_pt", 2 * n + 2))
                    o = bank[7][r, it * P:(it + 1) * P]
                    for w in range(2):
                        for jt in range(it + 1):
                            mm(o, vsw[w][:, jt, r], prt[:, n % 2, w, jt * P:(jt + 1) * P], start=w + jt == 0, stop=False)
                    mm(o, vcr[32 * tt:32 * tt + NCMP, r], pct[32 * tt:32 * tt + NCMP, g, it * P:(it + 1) * P],
                       start=False, stop=True).then_inc(sem["pv"], 1)

                for n in range(8 * NB):
                    for w in range(2):
                        if n + 1 < 8 * NB:
                            scores(n + 1, w)
                        pe.wait_ge(sem["s_p"], me.next("s_p"))
                        if n or w:
                            pe.wait_ge(sem["s_pt"], me.at("s_pt", 2 * n + w))
                        for jt in range(n % NB + 1):
                            i = pe.transpose(bank[6][:, jt * P:(jt + 1) * P], pr[:, n % 2, w, jt * P:(jt + 1) * P], ident)
                        i.then_inc(sem["s_t"], 1)
                        fill("pM1", PM1, (hp, hp), 4 + 2 * n + w)
                        if w == 0 and n:
                            values(n - 1)
                values(8 * NB - 1)
                for n in range(4):
                    if n >= 2:
                        pe.wait_ge(sem["vm_ready"], me.at("vm_ready", n - 1))
                    elif n == 1:
                        pe.wait_ge(sem["o_lo"], me.at("o_lo", 4))
                    transposes(bank[6 + n % 2], zm[:, 4 + n]).then_inc(sem["vm_mm"], 1)
                    if n:
                        fill("cb0", CB, (hp, op), n - 1)
                for n in range(3, 7):
                    fill("cb0", CB, (hp, op), n)
                pe.wait_ge(sem["row_m"], me.next("row_m"))
                pe.sem_inc(sem["held"], 1)
                for a in range(NB):
                    i = pe.transpose(bank[4][:, a * NH:(a + 1) * NH], row0[0:NH, a * P:(a + 1) * P], ident[0:NH, 0:NH])
                i.then_inc(sem["rt_mm"], 1)
                fill("cb0", CB, (hp, op), 7)
                pe.wait_ge(sem["vm_ready"], me.at("vm_ready", 4))
                pe.wait_ge(sem["rt_ready"], me.at("rt_ready", 1))
                pe.wait_ge(sem["cv_silu"], me.at("cv_silu", 4))
                sel = lambda h: con[0:NH, CCOLS["sel"] + h * P:CCOLS["sel"] + (h + 1) * P]
                for h in range(NH):
                    r = slice((h % 2) * HD, (h % 2 + 1) * HD)
                    q, k = zm[r, h // 2], zm[r, 2 + h // 2]
                    mm(bank[4][:], sel(h), rows[0:NH, 0], start=True, stop=True).then_inc(sem["mb_mm"], 1)
                    mm(bank[7][:], k[:, 0:P], q, start=True, stop=True).then_inc(sem["sm_mm"], 1)
                    if h:
                        pe.wait_ge(sem["h_out"], me.at("h_out", h))
                    mm(bank[5][:], sel(h), rows[0:NH, 0], start=True, stop=False)
                    mm(bank[5][:], identb, mask_ji.unsqueeze(1).broadcast_to([P, NB, P]), start=False, stop=True).then_inc(sem["md_mm"], 1)
                    mm(bank[6][:], sel(h), rows[0:NH, 1], start=True, stop=True).then_inc(sem["mm_mm"], 1)
                    fill("cb0", CB, (hp, op), 8 + 4 * h)
                    fill("cb0", CB, (hp, op), 9 + 4 * h)
                    pe.wait_ge(sem["d_exp"], me.next("d_exp"))
                    pe.wait_ge(sem["em_exp"], me.next("em_exp"))
                    mm(bank[6][:, 0:3 * P], k[:, P:2 * P], q[:, P:S], start=True, stop=True).then_inc(sem["sm_mm"], 1)
                    mm(bank[4][:, 0:2 * P], k[:, 2 * P:3 * P], q[:, 2 * P:S], start=True, stop=True)
                    mm(bank[4][:, 2 * P:3 * P], k[:, 3 * P:S], q[:, 3 * P:S], start=True, stop=True).then_inc(sem["sm_mm"], 1)
                    fill("cb0", CB, (hp, op), 10 + 4 * h)
                    for jt in range(NB):
                        pe.wait_ge(sem["sd_mul"], me.next("sd_mul"))
                        i = mm(bank[5][:, jt * P:S], zm[:, 4 + h, jt * P:(jt + 1) * P], dm[jt], start=jt == 0, stop=jt == NB - 1)
                    i.then_inc(sem["num_mm"], 1)
                    for jt in range(NB):
                        i = mm(bank[6][:, jt * P:S], ones[:], dm[jt], start=jt == 0, stop=jt == NB - 1)
                    i.then_inc(sem["den_mm"], 1)
                    fill("cb0", CB, (hp, op), 11 + 4 * h)
                pe.wait_ge(sem["h_out"], me.at("h_out", 4))
                for p in range(2):
                    mm(bank[4 + p][:], cur[R_LR:R_LR + 16, COLS["walpha"] + p * P:COLS["walpha"] + (p + 1) * P],
                       small[R_LR:R_LR + 16], start=True, stop=True).then_inc(sem["al_mm"], 1)
                for h in range(NH):
                    if h >= 2:
                        fill("cb1", CB, (hp, op), h - 2)
                        pe.wait_ge(sem["vg_ready"], me.at("vg_ready", h - 1))
                    transposes(bank[6 + h % 2], zm[:, 16 + h]).then_inc(sem["vg_mm"], 1)
                pe.wait_ge(sem["o_lo"], me.at("o_lo", 8))
                fill("cb1", CB, (hp, op), 2)
                fill("cb1", CB, (hp, op), 3)
                pe.wait_ge(sem["vg_ready"], me.at("vg_ready", 4))
                pe.wait_ge(sem["al_b"], me.at("al_b", 2))
                pe.wait_ge(sem["ad_zero"], me.at("ad_zero", 1))
                for p in range(2):
                    for v in range(len(LEVELS) + 1):
                        s = LEVELS[v] if v < len(LEVELS) else 0
                        if s:
                            fill("cb1", CB, (hp, op), 4 + 11 * p + v)
                            pe.wait_ge(sem["lv_m"], me.next("lv_m"))
                        if v in (2, 3):
                            pe.wait_ge(sem["lv_rect"], me.at("lv_rect", 4 * p + 2 * (v - 1)))
                        elif v >= 4:
                            pe.wait_ge(sem["lv_out"], me.at("lv_out", 16 * p + 2 * (v - 3)))
                        elif p:
                            pe.wait_ge(sem["og_t"], me.at("og_t", 2))
                        for hh in range(2):
                            r = slice(hh * HD, (hh + 1) * HD)
                            b = bank[4 + 2 * (v % 2) + hh]
                            M = tmp[r, 2 + v % 2]
                            a, c = (M, M) if s else (zm[r, 14 + p], zm[r, 12 + p])
                            if s == 2 * P:
                                for jt in range(2):
                                    i = mm(b[:, jt * 2 * P:(jt + 1) * 2 * P], a[:, jt * P:(jt + 1) * P], c[:, 2 * P:S],
                                           start=True, stop=True)
                            elif s == P:
                                for jt in range(2):
                                    i = mm(b[:, jt * P:(jt + 1) * P], a[:, 2 * jt * P:(2 * jt + 1) * P],
                                           c[:, (2 * jt + 1) * P:(2 * jt + 2) * P], start=True, stop=True)
                            else:
                                for jt in range(NB):
                                    i = mm(b[:, jt * P:(jt + 1) * P], a[:, jt * P:(jt + 1) * P], c[:, jt * P:(jt + 1) * P],
                                           start=True, stop=True)
                        i.then_inc(sem["lv_mm"], 1)
                    for hh in range(2):
                        h = 2 * p + hh
                        if hh == 0:
                            pe.wait_ge(sem["lv_out"], me.at("lv_out", 16 * (p + 1)))
                            pe.wait_ge(sem["lv_rect"], me.at("lv_rect", 4 * (p + 1)))
                        for jt in range(NB):
                            o, v_ = bank[4 + hh][:], zm[:, 16 + h, jt * P:(jt + 1) * P]
                            i = mm(o[:, jt * P:(jt + 1) * P], v_, ad[:, hh, jt], start=jt == 0, stop=jt == NB - 1)
                            if jt < NB - 1:
                                mm(o[:, (jt + 1) * P:S], v_, ao[:, hh, jt, 0:S - (jt + 1) * P], start=False, stop=False)
                        i.then_inc(sem["og_mm"], 1)
                    for hh in range(2):
                        if p == 0:
                            fill("cb1", CB, (hp, op), 13 + hh)
                        else:
                            for k in range(hh * KD // 2, (hh + 1) * KD // 2):
                                step(2 * FIRST["cb2"], 0, bank[0][:], hp, k, free=FIRST["cb2"] - 1)
                        pe.wait_ge(sem["og_sq"], me.next("og_sq"))
                        if hh:
                            pe.wait_ge(sem["og_ln"], me.at("og_ln", 2 * p + hh))
                        mm(bank[6][:], onesm[:], tmp[:, 2], start=True, stop=True).then_inc(sem["og_ss"], 1)
                section("cb2", hp, op, started=True, ready=("o_lo", 8))
                section("wo", yp, yp, ready=("ylo_ready", 0))
                norm(2)
                ffn(1)


def kernel(**a):
    import numpy as np
    import ml_dtypes
    import concourse.bacc as _bacc
    from concourse.bass_utils import run_bass_kernel_spmd as _run
    a = {k: np.asarray(v) for k, v in a.items()}

    def tiles(w):
        l, k, m = w.shape
        return w.reshape(l, k // P, P, m // P, P).transpose(0, 3, 2, 1, 4).reshape(l, m // P, P, k)

    def pairs(w):
        l, n, p, k = w.shape
        return w.reshape(l, n // 2, 2, p, k).transpose(0, 1, 3, 2, 4).reshape(l, n // 2, p, 2 * k)

    arr = {"xT": np.ascontiguousarray(a["x"][0].T)}
    for f in (0, 1):
        g, u = tiles(a[f"ffn{f + 1}_w_gate"]), tiles(a[f"ffn{f + 1}_w_up"])
        arr[f"gu{f}"] = np.concatenate([g, u], 3)
        arr[f"dn{f}"] = tiles(a[f"ffn{f + 1}_w_down"])
    sizes = [256, 256, 512, 512, 16, 512] + [128] * 6 + [24, 512, 512, 512, 4, 4, DM, DM, DM]
    off = np.concatenate([[0], np.cumsum(sizes)])
    names = ["aq", "ak", "av", "ar", "alr", "bq", "bkc", "bvc", "bks", "bvs", "bkw", "bvw", "bg", "cqk", "cv", "co",
             "ci", "cf", "ga", "gb", "gc"]
    at = {n: np.arange(off[i], off[i + 1]) for i, n in enumerate(names)}
    small = np.full(P, -1)
    small[R_F:R_F + 4], small[R_I:R_I + 4], small[R_LR:R_LR + 16], small[R_G:R_G + 24] = at["cf"], at["ci"], at["alr"], at["bg"]
    pair = np.concatenate([np.concatenate([np.arange(h * HD, (h + 1) * HD), np.arange((h + 4) * HD, (h + 5) * HD)])
                           for h in range(4)])
    order = {"pA": [small, at["bvs"], at["bvw"], at["bkc"], at["bvc"], at["bq"][pair], at["bks"], at["bkw"], np.full(P, -1)],
             "pM": [at["cqk"], at["cv"], at["co"], at["aq"], at["ak"], at["av"], at["ar"]]}
    w_in = np.concatenate([a["w_in"], np.zeros((L, DM, 1), np.float32)], 2)
    b_in = np.concatenate([a["b_in"], np.zeros((L, 1), np.float32)], 1)
    cols = lambda v: v.reshape(v.shape[0], -1, P).transpose(0, 2, 1)
    bias = []
    for name, idx in order.items():
        idx = np.concatenate(idx)
        arr[name] = pairs(tiles(w_in[:, :, idx]))
        bias.append(cols(b_in[:, idx]))
    w1 = a["nsa_cmp_w1"].reshape(L, 2, 16, P, 2, P).transpose(0, 1, 4, 3, 2, 5)
    pm = arr.pop("pM")
    arr["pM0"], arr["pM1"] = pm[:, 0:2], pm[:, 6:12]
    arr["cq"] = np.stack([w1.reshape(L, 4, P, 16 * P), pm[:, 2:6]], 2).reshape(L, 8, P, 16 * P)
    branch = [a["w_branch"][:, 1][:, pair], a["w_branch"][:, 2], a["w_branch"][:, 0]]
    gates = [at["gb"], at["gc"], at["ga"]]
    for b in range(3):
        arr[f"cb{b}"] = np.concatenate([tiles(a["w_in"][:, :, gates[b]]), tiles(branch[b])], 3)
    arr["wo"] = pairs(tiles(a["w_out"]))
    walpha = np.zeros((L, P, 256), np.float32)
    walpha[:, R_LR:R_LR + 16] = a["gla_w_alpha"]
    params = [cols(a["ffn1_norm"]), cols(a["mix_norm"]), cols(a["ffn2_norm"]), *bias, *[cols(a["b_in"][:, g]) for g in gates],
              a["mlstm_conv_w"].reshape(L, 4, 4, P).transpose(0, 3, 2, 1).reshape(L, P, 16), cols(a["mlstm_conv_b"]),
              np.concatenate([a["nsa_qk_norm"]] * 2, 2).transpose(0, 2, 1), a["gla_out_norm"][:, :, None], cols(a["gla_b_alpha"]),
              a["nsa_cmp_pos"].reshape(L, 2, 16, P).transpose(0, 3, 1, 2).reshape(L, P, 32),
              a["nsa_cmp_w2"].reshape(L, 2, 2, P, HD).transpose(0, 3, 1, 2, 4).reshape(L, P, 256), walpha]
    arr["params"] = np.concatenate(params, 2)
    half = HD // 2
    freqs = np.float32(10000.0) ** (-np.arange(half, dtype=np.float32) / np.float32(half))
    fr = np.tile(freqs, 4)[:, None].astype(np.float32)
    ang = fr * np.arange(S, dtype=np.float32)[None]
    cang = fr * (np.arange(32, dtype=np.float32)[None] * CS + 2 * CS - 1)
    rot = np.zeros((P, P), np.float32)
    for q in range(0, P, HD):
        for i in range(half):
            rot[q + half + i, q + i] = -1.0
            rot[q + i, q + half + i] = 1.0
    r = np.arange(P)
    blk = (r[:, None] // HD == r[None] // HD) / np.float32(HD)
    sel = np.zeros((P, NH * P), np.float32)
    for h in range(NH):
        sel[h, h * P:(h + 1) * P] = 1.0
    arr["con"] = np.concatenate([np.eye(P), rot, blk, np.cos(ang), np.sin(ang), np.cos(cang), np.sin(cang), sel], 1).astype(np.float32)
    later = np.where(r[None] > r[:, None], -1e30, 0.0)
    tok = np.arange(S).reshape(NB, P).T
    cend = np.arange(NCMP) * CS + 2 * CS - 1
    cm = np.where(cend[None, None] > tok[:, :, None], -1e30, 0.0).reshape(P, -1)
    arr["conb"] = np.concatenate([np.eye(P), later, -later.T, cm, np.zeros((P, 4))], 1).astype(ml_dtypes.bfloat16)
    j, i = r[:, None], r[None]
    lv = [(j // (2 * s) == i // (2 * s)) & (j % (2 * s) < s) & (i % (2 * s) >= s) for s in LEVELS[2:]] + [j == i]
    arr["masks"] = np.stack(lv, 1).astype(np.float32)
    arr = {k: np.ascontiguousarray(v) for k, v in arr.items()}
    nc = _bacc.Bacc("TRN2", target_bir_lowering=False, num_devices=1)
    t = {k: nc.dram_tensor(k, v.shape, mybir.dt.from_np(v.dtype), kind="ExternalInput").ap() for k, v in arr.items()}
    o = nc.dram_tensor("outT", (DM, S), f32, kind="ExternalOutput").ap()
    build(nc, t, o)
    got = _run(nc, [arr], core_ids=[0])
    return np.ascontiguousarray(got.results[0]["outT"].T)[None]
```
